# Optimizing a Trainium2 kernel written in Bass

```python
import jax
import jax.numpy as jnp
from jax import lax
import numpy as np

D_MODEL = 1024
BATCH = 1
SEQ = 128
DEPTH = 2
DEC_BATCH = 1
DEC_SEQ = 512
PAST_LEN = 128

GRID_W = 64
N_EVEN = (DEPTH + 1) // 2
N_ODD = DEPTH // 2
N_ATTN_LAYERS = N_EVEN
N_MOD = 6
EPS = 1e-6

CONV_WIDTH = 512
CONV_KERNEL = 31
N_HEADS = 8
N_KV_HEADS = 2
HEAD_DIM = 64
ATTN_WIDTH = N_HEADS * HEAD_DIM
KV_WIDTH = N_KV_HEADS * HEAD_DIM
Q_BLOCK = 128
ROPE_THETA = 10000.0
FOURIER_GROUPS = 4
FOURIER_GROUP_DIM = 128
FOURIER_WIDTH = FOURIER_GROUPS * FOURIER_GROUP_DIM
SHORT_WIDTH = 512
SHORT_KERNEL = 3

EVEN_IN = 2 * CONV_WIDTH + ATTN_WIDTH + 2 * KV_WIDTH
EVEN_OUT = CONV_WIDTH + ATTN_WIDTH
ODD_IN = FOURIER_WIDTH + 3 * SHORT_WIDTH
ODD_OUT = FOURIER_WIDTH + SHORT_WIDTH

PEER_HEADS = 8
PEER_KEYS = 128
PEER_EXPERTS = PEER_KEYS * PEER_KEYS
PEER_QDIM = 256
PEER_HALF = PEER_QDIM // 2
PEER_TOPK = 16
PEER_TOKEN_BLOCK = 128

kernel_name = 'hybrid_diffusion_prefix_trunk_step'

def rms_norm(x, g):
    xf = x.astype(jnp.float32)
    y = xf * lax.rsqrt(jnp.mean(xf * xf, axis=-1, keepdims=True) + EPS)
    return (y * g.astype(jnp.float32)).astype(x.dtype)

def layer_norm(x, g, b):
    xf = x.astype(jnp.float32)
    mu = jnp.mean(xf, axis=-1, keepdims=True)
    xc = xf - mu
    var = jnp.mean(xc * xc, axis=-1, keepdims=True)
    y = xc * lax.rsqrt(var + EPS) * g.astype(jnp.float32) + b.astype(jnp.float32)
    return y.astype(x.dtype)

def depthwise_conv(x, w):
    return lax.conv_general_dilated(x, w[:, None, :], window_strides=(1,), padding='SAME',
                                    dimension_numbers=('NWC', 'WIO', 'NWC'),
                                    feature_group_count=x.shape[-1])

def axial_rope_tables(n_tokens):
    rows = n_tokens // GRID_W
    row = jnp.repeat(jnp.arange(rows), GRID_W).astype(jnp.float32)
    col = jnp.tile(jnp.arange(GRID_W), rows).astype(jnp.float32)
    half = HEAD_DIM // 2
    inv = ROPE_THETA ** (-jnp.arange(0, half, 2, dtype=jnp.float32) / half)
    ang = jnp.concatenate([row[:, None] * inv, col[:, None] * inv], axis=-1)
    return jnp.cos(ang), jnp.sin(ang)

def apply_rope(x, cos, sin):
    xf = x.astype(jnp.float32).reshape(*x.shape[:-1], HEAD_DIM // 2, 2)
    x1, x2 = xf[..., 0], xf[..., 1]
    cc = cos[None, :, None, :]
    ss = sin[None, :, None, :]
    out = jnp.stack([x1 * cc - x2 * ss, x1 * ss + x2 * cc], axis=-1)
    return out.reshape(x.shape).astype(x.dtype)

def block_attention(q, k, v):
    b, tq = q.shape[0], q.shape[1]
    grp = N_HEADS // N_KV_HEADS
    nblk = tq // Q_BLOCK
    qb = jnp.moveaxis(q.reshape(b, nblk, Q_BLOCK, N_KV_HEADS, grp, HEAD_DIM), 1, 0)
    kf = k.astype(jnp.float32)
    vf = v.astype(jnp.float32)
    scale = HEAD_DIM ** -0.5

    def one_block(qblk):
        s = jnp.einsum('bqkgd,bskd->bkgqs', qblk.astype(jnp.float32), kf) * scale
        p = jax.nn.softmax(s, axis=-1)
        return jnp.einsum('bkgqs,bskd->bqkgd', p, vf).astype(q.dtype)

    o = lax.map(one_block, qb)
    return jnp.moveaxis(o, 0, 1).reshape(b, tq, ATTN_WIDTH)

def even_mixer(h, p, ctx_k, ctx_v, rope):
    b, t, _ = h.shape
    proj = h @ p['w_in']
    s1 = CONV_WIDTH
    s2 = 2 * CONV_WIDTH
    s3 = s2 + ATTN_WIDTH
    s4 = s3 + KV_WIDTH
    a_val, a_gate, q, k, v = jnp.split(proj, [s1, s2, s3, s4], axis=-1)
    a = a_val * jax.nn.sigmoid(a_gate)
    a = depthwise_conv(a, p['conv_w']) + p['conv_b']
    a = jax.nn.silu(layer_norm(a, p['ln_g'], p['ln_b']))
    q = rms_norm(q.reshape(b, t, N_HEADS, HEAD_DIM), p['q_g'])
    k = rms_norm(k.reshape(b, t, N_KV_HEADS, HEAD_DIM), p['k_g'])
    v = v.reshape(b, t, N_KV_HEADS, HEAD_DIM)
    if rope is None:
        attn = block_attention(q, k, v)
    else:
        cos, sin = rope
        q = apply_rope(q, cos, sin)
        k = apply_rope(k, cos, sin)
        attn = block_attention(q, jnp.concatenate([ctx_k, k], axis=1),
                               jnp.concatenate([ctx_v, v], axis=1))
    out = jnp.concatenate([a, attn], axis=-1) @ p['w_out']
    return out, k, v

def odd_mixer(h, p):
    b, t, _ = h.shape
    proj = h @ p['w_in']
    f, g_b, g_c, hv = jnp.split(proj, [FOURIER_WIDTH, FOURIER_WIDTH + SHORT_WIDTH,
                                       FOURIER_WIDTH + 2 * SHORT_WIDTH], axis=-1)
    ff = f.reshape(b, t, FOURIER_GROUPS, FOURIER_GROUP_DIM).astype(jnp.float32)
    ff = jnp.fft.fft2(ff, axes=(1, 3), norm='ortho').real
    ff = ff.astype(h.dtype).reshape(b, t, FOURIER_WIDTH)
    sd = g_b * depthwise_conv(g_c * hv, p['short_w'])
    return jnp.concatenate([ff, sd], axis=-1) @ p['w_out']

def peer(h, wq, keys, u_tab, v_tab):
    b, t, d = h.shape
    blocks = h.reshape(-1, PEER_TOKEN_BLOCK, d)
    keys_f = keys.astype(jnp.float32)

    def one_block(xb):
        n = xb.shape[0]
        q = (xb @ wq).reshape(n, PEER_HEADS, 2, PEER_HALF).astype(jnp.float32)
        s = jnp.einsum('nhpd,hpkd->nhpk', q, keys_f)
        sv, si = lax.top_k(s, PEER_TOPK)
        cand = sv[:, :, 0, :, None] + sv[:, :, 1, None, :]
        cidx = si[:, :, 0, :, None] * PEER_KEYS + si[:, :, 1, None, :]
        cand = cand.reshape(n, PEER_HEADS, PEER_TOPK * PEER_TOPK)
        cidx = cidx.reshape(n, PEER_HEADS, PEER_TOPK * PEER_TOPK)
        fv, fi = lax.top_k(cand, PEER_TOPK)
        eidx = jnp.take_along_axis(cidx, fi, axis=-1)
        gate = jax.nn.softmax(fv, axis=-1)
        ue = jnp.take(u_tab, eidx, axis=0)
        act = jax.nn.gelu(jnp.einsum('nhkd,nd->nhk', ue, xb).astype(jnp.float32))
        ve = jnp.take(v_tab, eidx, axis=0)
        return jnp.einsum('nhk,nhkd->nd', (gate * act).astype(xb.dtype), ve)

    return lax.map(one_block, blocks).reshape(b, t, d)

def modulate(x, g, shift, scale):
    return rms_norm(x, g) * (1 + scale) + shift

def setup_inputs(seed: int = 0) -> dict:
    key = jax.random.key(seed)
    ks = jax.random.split(key, 32)
    f32 = jnp.float32

    def nrm(k, shape, scale):
        return jax.random.normal(k, shape, f32) * scale

    def gain(k, shape):
        return 1.0 + 0.01 * jax.random.normal(k, shape, f32)

    cache_shape = (DEC_BATCH, N_ATTN_LAYERS, PAST_LEN, N_KV_HEADS, HEAD_DIM)
    return {
        'x_prompt': nrm(ks[0], (BATCH, SEQ, D_MODEL), 1.0),
        'x_sample': nrm(ks[1], (DEC_BATCH, DEC_SEQ, D_MODEL), 1.0),
        'cache_k': nrm(ks[2], cache_shape, 1.0),
        'cache_v': nrm(ks[3], cache_shape, 1.0),
        'c': nrm(ks[4], (DEC_BATCH, D_MODEL), 1.0),
        'c_ctx': nrm(ks[5], (D_MODEL,), 1.0),
        'w_mod': nrm(ks[6], (DEPTH, D_MODEL, N_MOD * D_MODEL), 0.5 * D_MODEL ** -0.5),
        'b_mod': nrm(ks[7], (DEPTH, N_MOD * D_MODEL), 0.01),
        'norm_mix_g': gain(ks[8], (DEPTH, D_MODEL)),
        'norm_ffn_g': gain(ks[9], (DEPTH, D_MODEL)),
        'w_in_even': nrm(ks[10], (N_EVEN, D_MODEL, EVEN_IN), D_MODEL ** -0.5),
        'w_out_even': nrm(ks[11], (N_EVEN, EVEN_OUT, D_MODEL), EVEN_OUT ** -0.5),
        'conv_dw_w': nrm(ks[12], (N_EVEN, CONV_KERNEL, CONV_WIDTH), CONV_KERNEL ** -0.5),
        'conv_dw_b': nrm(ks[13], (N_EVEN, CONV_WIDTH), 0.01),
        'conv_ln_g': gain(ks[14], (N_EVEN, CONV_WIDTH)),
        'conv_ln_b': nrm(ks[15], (N_EVEN, CONV_WIDTH), 0.01),
        'q_norm_g': gain(ks[16], (N_EVEN, HEAD_DIM)),
        'k_norm_g': gain(ks[17], (N_EVEN, HEAD_DIM)),
        'w_in_odd': nrm(ks[18], (N_ODD, D_MODEL, ODD_IN), D_MODEL ** -0.5),
        'w_out_odd': nrm(ks[19], (N_ODD, ODD_OUT, D_MODEL), ODD_OUT ** -0.5),
        'short_conv_w': nrm(ks[20], (N_ODD, SHORT_KERNEL, SHORT_WIDTH), SHORT_KERNEL ** -0.5),
        'peer_wq': nrm(ks[21], (DEPTH, D_MODEL, PEER_HEADS * PEER_QDIM), D_MODEL ** -0.5),
        'peer_keys': nrm(ks[22], (DEPTH, PEER_HEADS, 2, PEER_KEYS, PEER_HALF), PEER_HALF ** -0.5),
        'peer_u': nrm(ks[23], (DEPTH, PEER_EXPERTS, D_MODEL), D_MODEL ** -0.5),
        'peer_v': nrm(ks[24], (DEPTH, PEER_EXPERTS, D_MODEL), 0.5),
        'final_norm_g': gain(ks[25], (D_MODEL,)),
    }

def reference(x_prompt, x_sample, cache_k, cache_v, c, c_ctx, w_mod, b_mod, norm_mix_g, norm_ffn_g,
              w_in_even, w_out_even, conv_dw_w, conv_dw_b, conv_ln_g, conv_ln_b, q_norm_g, k_norm_g,
              w_in_odd, w_out_odd, short_conv_w, peer_wq, peer_keys, peer_u, peer_v, final_norm_g):
    rope = axial_rope_tables(x_sample.shape[1])

    def modulation(l, cond):
        m = jax.nn.silu(cond) @ w_mod[l] + b_mod[l]
        return m.reshape(cond.shape[0], 1, N_MOD, D_MODEL)

    xc = x_prompt
    xs = x_sample
    new_k = []
    new_v = []
    for l in range(DEPTH):
        mc = modulation(l, c_ctx[None, :])
        ms = modulation(l, c)
        hc = modulate(xc, norm_mix_g[l], mc[:, :, 0], mc[:, :, 1])
        hs = modulate(xs, norm_mix_g[l], ms[:, :, 0], ms[:, :, 1])
        if l % 2 == 0:
            j = l // 2
            p = {'w_in': w_in_even[j], 'w_out': w_out_even[j], 'conv_w': conv_dw_w[j],
                 'conv_b': conv_dw_b[j], 'ln_g': conv_ln_g[j], 'ln_b': conv_ln_b[j],
                 'q_g': q_norm_g[j], 'k_g': k_norm_g[j]}
            oc, kc, vc = even_mixer(hc, p, None, None, None)
            new_k.append(kc)
            new_v.append(vc)
            o_s, _, _ = even_mixer(hs, p, cache_k[:, j], cache_v[:, j], rope)
        else:
            j = l // 2
            p = {'w_in': w_in_odd[j], 'w_out': w_out_odd[j], 'short_w': short_conv_w[j]}
            oc = odd_mixer(hc, p)
            o_s = odd_mixer(hs, p)
        xc = xc + mc[:, :, 2] * oc
        xs = xs + ms[:, :, 2] * o_s
        hc = modulate(xc, norm_ffn_g[l], mc[:, :, 3], mc[:, :, 4])
        hs = modulate(xs, norm_ffn_g[l], ms[:, :, 3], ms[:, :, 4])
        xc = xc + mc[:, :, 5] * peer(hc, peer_wq[l], peer_keys[l], peer_u[l], peer_v[l])
        xs = xs + ms[:, :, 5] * peer(hs, peer_wq[l], peer_keys[l], peer_u[l], peer_v[l])
    y_prompt = rms_norm(xc, final_norm_g)
    y_sample = rms_norm(xs, final_norm_g)
    new_cache_k = jnp.stack(new_k, axis=1)
    new_cache_v = jnp.stack(new_v, axis=1)
    return (y_prompt, y_sample, new_cache_k, new_cache_v)


_drawn_inputs = setup_inputs


def setup_inputs(seed=0):
    import zlib

    import numpy as np

    out = dict(_drawn_inputs(seed))
    spreads = {}
    factors = {'cache_k': 5.205,
     'cache_v': 4.702,
     'norm_mix_g': 5.815,
     'norm_ffn_g': 26.031,
     'conv_dw_b': 7.739,
     'conv_ln_g': 97.827,
     'conv_ln_b': 87.942,
     'q_norm_g': 8.0,
     'k_norm_g': 5.77,
     'final_norm_g': 171.949}
    for name, (base, spread) in spreads.items():
        noise = np.random.default_rng([zlib.crc32(name.encode()), seed]).standard_normal(out[name].shape)
        drawn = base * np.exp(spread * noise) if base else spread * noise
        out[name] = jnp.asarray(drawn.astype(out[name].dtype))
    for name, factor in factors.items():
        out[name] = (out[name] * factor).astype(out[name].dtype)
    return out
```

```python
from contextlib import ExitStack

import numpy as np
import concourse.bass as bass
from concourse import mybir

F32 = mybir.dt.float32
U32 = mybir.dt.uint32
ALU = mybir.AluOpType
ACT = mybir.ActivationFunctionType
AX = mybir.AxisListType.X

P = 128
D = 1024
DC = D // P
NB = 5
HEADS = 8
TOPK = 16
KEYS = 128
EXPERTS = KEYS * KEYS
EPS = 1e-6
NU = 8
NV = 8
NW = 3
WC = 256
NDIAG = 4
NEG = -3.0e38
CONVK = 31
CW_ROWS = CONVK + 3
PAD = CONVK // 2
HD = 64
QK = 640
BOX = 1024
CTX, SMP = 0, 1
BLOCKS = {CTX: [0], SMP: [1, 2, 3, 4]}


def plan_boxes():
    keys = []

    def mod(l):
        keys.append(("condT", l))
        keys.append(("mod", l))
        keys.append(("modT", l))

    def mix(l, g):
        nb = len(BLOCKS[g])
        keys.append(("cwT", l, g))
        for b in range(nb):
            keys.append(("hT", l, g, b))
        if l == 0:
            for c in range(4):
                keys.append(("vg", g, c))
            if g == SMP:
                keys.append(("ckT", g))
            for b in range(nb):
                keys.append(("qkv", g, b))
                keys.append(("qkT", g, b))
            n = 0
            for b in range(nb):
                for h in range(HEADS):
                    keys.append(("S", g, b, h))
                    keys.append(("PT", g, b, h))
                    keys.append(("O", g, b, h))
                keys.append(("oT", g, b))
            keys.append(("mean", g))
            keys.append(("var", g))
        else:
            for c in range(4):
                keys.append(("fT", g, c))
            for c in range(4):
                keys.append(("cv", g, c))
                keys.append(("gb", g, c))
            for b in range(nb):
                keys.append(("Y", g, b))
            for c in range(4):
                keys.append(("ffT", g, c))
        for s in range(4):
            for b in range(nb):
                keys.append(("out", l, g, s, b))
        for b in range(nb):
            keys.append(("h2T", l, g, b))
        for s in range(8):
            keys.append(("kyT", l, g, s))
            for j in range(2):
                keys.append(("q", l, g, 2 * s + j))
                keys.append(("sc", l, g, 2 * s + j))

    mod(0)
    mix(0, CTX)
    mix(0, SMP)
    mod(1)
    mix(1, CTX)
    mix(1, SMP)
    return {k: (n % 3, n // 3) for n, k in enumerate(keys)}


def plan_weights():
    order = []

    def mod(l):
        for s in range(24):
            order.append((("wmod", l, s), ("mod", l), 1))

    def mix(l, g):
        nb = len(BLOCKS[g])
        if l == 0:
            for s, c in ((0, 1), (2, 1), (1, 3), (3, 3)):
                order.append((("win", l, g, s), ("vg", g, c), 1))
            for s in (4, 5, 6):
                order.append((("win", l, g, s), ("qkv", g, nb - 1), 1))
        else:
            for s in (0, 1):
                order.append((("win", l, g, s), ("fT", g, 2 * s + 1), 1))
            for half in (0, 1):
                for s in (2, 4, 6):
                    order.append((("win", l, g, s + half), ("gb", g, 2 * half + 1), 1))
        for s in range(4):
            order.append((("wout", l, g, s), ("out", l, g, s, nb - 1), 1))
        for s in range(8):
            order.append((("wq", l, g, s), ("q", l, g, 2 * s + 1), 2))

    mod(0)
    mix(0, CTX)
    mix(0, SMP)
    mod(1)
    mix(1, CTX)
    mix(1, SMP)
    plan, counts = {}, [0] * NW
    for n, (key, last, dmas) in enumerate(order):
        slot = n % NW
        counts[slot] += 16 * dmas
        before = order[n - NW] if n >= NW else None
        plan[key] = (slot, counts[slot], before)
    return plan


def build(nc, T, outs):
    boxes = plan_boxes()
    weights = plan_weights()
    y_prompt, y_sample, new_k, new_v = outs

    with ExitStack() as ctx:
        def sb(name, shape, dt=F32):
            return ctx.enter_context(nc.sbuf_tensor(name, shape, dt))

        def sem(name):
            return ctx.enter_context(nc.semaphore(name))

        def dram(name, shape):
            return nc.dram_tensor(name, shape, F32, kind="Internal").ap()

        modrow = dram("modrow", [2, 2, 6, D])
        xa = dram("xa", [10, P, D])
        xb = dram("xb", [5, P, D])
        hs = dram("hs", [10, P, D])
        sc = dram("sc", [80, P, 2, KEYS])

        ident = sb("ident", [P, P])
        ones = sb("ones", [P, P])
        dft_ch = sb("dft_ch", [P, 2 * P])
        rope = sb("rope", [P, 4, 2, 32])
        iota16 = sb("iota16", [P, 16])
        eps = sb("eps", [P, 1])
        u_ring = sb("u_ring", [P, NU, D])
        v_ring = sb("v_ring", [P, NV, D])
        w_slots = sb("w_slots", [P, NW, DC * WC + 2 * P])
        h_cur = sb("h_cur", [P, D])
        h_next = sb("h_next", [P, D])
        x_seg = sb("x_seg", [P, D])
        g_seg = sb("g_seg", [P, D])
        t_seg = sb("t_seg", [P, D])
        s_buf = sb("s_buf", [P, 2, 2, KEYS])
        diag = sb("diag", [P, NDIAG, P])
        sv = sb("sv", [P, 2, TOPK])
        si = sb("si", [P, 2, TOPK], U32)
        sif = sb("sif", [P, 2, TOPK])
        cand = sb("cand", [P, 16, 16])
        fv = sb("fv", [P, 2, TOPK])
        fi = sb("fi", [P, TOPK], U32)
        ab = sb("ab", [P, 2, TOPK], U32)
        abf = sb("abf", [P, 2, TOPK])
        onehot = sb("onehot", [P, 2, 16, 16])
        cand_rep = onehot[:, 0].rearrange("p a b -> p (a b)")
        s_rep = onehot[:, 1].rearrange("p a (h b) -> p (a h b)", h=1).rearrange("p (j k) -> p j k", j=2)
        e01 = sb("e01", [P, 2, TOPK])
        neg_max = sb("neg_max", [P, 2])
        idx = sb("idx", [P, 4, TOPK], U32)
        ex = sb("ex", [P, 4, TOPK])
        ex_sum = sb("ex_sum", [P, 4])
        ex_rec = sb("ex_rec", [P, 4])
        act_v = sb("act_v", [P, 2, TOPK])
        gelu_v = sb("gelu_v", [P, 2, TOPK])
        w_v = sb("w_v", [P, 2, TOPK])
        seg_st = sb("seg_st", [P, 4])
        XM = sb("XM", [P, 4, D])
        HT = sb("HT", [P, 4096])
        CAT = sb("CAT", [P, 4096])
        BC = sb("BC", [P, 2, D])
        AR = sb("AR", [P, 7300])
        st = sb("st", [P, 64])

        ps_v = ctx.enter_context(nc.psum_tensor("ps_v", [P, D], F32))
        ps_box = [ctx.enter_context(nc.psum_tensor(f"ps_box{i}", [P, BOX], F32)) for i in range(3)]

        const_in = sem("const_in")
        iota_set = sem("iota_set")
        u_landed = [sem(f"u_landed{i}") for i in range(NU)]
        v_landed = [sem(f"v_landed{i}") for i in range(NV)]
        dots_done = sem("dots_done")
        vsum_done = sem("vsum_done")
        acc_free = sem("acc_free")
        s_landed = [sem("s_landed0"), sem("s_landed1")]
        topk_done = sem("topk_done")
        negmax_done = sem("negmax_done")
        exp_done = sem("exp_done")
        gelu_done = sem("gelu_done")
        w_done = sem("w_done")
        diag_done = sem("diag_done")
        h_landed = sem("h_landed")
        h_ready = sem("h_ready")
        seg_landed = sem("seg_landed")
        x_new = sem("x_new")
        ss_done = sem("ss_done")
        y_new = sem("y_new")
        x_stored = sem("x_stored")
        fg_landed = sem("fg_landed")
        dve_chain = sem("dve_chain")
        act_chain = sem("act_chain")
        box_ready = [sem(f"box_ready{i}") for i in range(3)]
        box_free = [sem(f"box_free{i}") for i in range(3)]
        w_landed = [sem(f"w_landed{i}") for i in range(NW)]

        named = {}

        def S(*key):
            name = "_".join(str(k) for k in key)
            if name not in named:
                named[name] = sem(name)
            return named[name]

        def wait(eng, s, n, use=""):
            if isinstance(n, int):
                if n > 0:
                    eng.wait_ge(s, n)
            else:
                n.loop.wait(s, n, use)

        class Count:
            def __init__(self, loop, per_seg, base):
                self.loop, self.per_seg, self.base = loop, per_seg, base

            def __add__(self, n):
                return Count(self.loop, self.per_seg, self.base + n)

            def __sub__(self, n):
                return self + -n

            def __mul__(self, n):
                return Count(self.loop, self.per_seg * n, self.base * n)

            __radd__, __rmul__ = __add__, __mul__

            def value(self):
                return self.loop.seg * self.per_seg + self.base

        class Segments:
            def __init__(self, eng, lo, hi, counts):
                self.eng, self.lo, self.hi, self.counts = eng, lo, hi, counts

            def __enter__(self):
                self.at = {}
                for key, (per_seg, first) in self.counts.items():
                    if per_seg * self.lo + first > 0:
                        reg = self.eng.alloc_register(f"{key[0].name}_{key[1]}_{self.lo}_wanted")
                        self.eng.reg_mov(reg, per_seg * self.lo + first)
                        self.at[key] = [reg, first]
                self.fori = self.eng.Fori(self.lo, self.hi)
                self.seg = self.fori.__enter__()
                return Count(self, 1, 0)

            def wait(self, s, n, use):
                per_seg, _ = self.counts[s, use]
                reg, at = self.at[s, use]
                assert n.per_seg == per_seg and n.base >= at
                if n.base != at:
                    self.eng.reg_add(reg, reg, n.base - at)
                self.eng.wait_ge(s, reg)
                self.eng.reg_add(reg, reg, 1)
                self.at[s, use][1] = n.base + 1

            def __exit__(self, *exc):
                for key, (reg, at) in self.at.items():
                    per_seg, first = self.counts[key]
                    if at not in (first, first + per_seg):
                        self.eng.reg_add(reg, reg, per_seg + first - at)
                return self.fori.__exit__(*exc)

        class Chain:
            def __init__(self, eng, s):
                self.eng, self.s, self.n = eng, s, 0

            def __call__(self, ins):
                self.n += 1
                ins.then_inc(self.s, 1)
                self.eng.wait_ge(self.s, self.n)

            def restart(self):
                self.eng.sem_clear(self.s)
                self.n = 0

        def index(n):
            return n if isinstance(n, int) else n.value()

        def fill(pe, key):
            box, use = boxes[key]
            if use:
                pe.wait_ge(box_free[box], use)
            return ps_box[box]

        def filled(ins, key):
            ins.then_inc(box_ready[boxes[key][0]], 1)

        def take(eng, key):
            box, use = boxes[key]
            eng.wait_ge(box_ready[box], use + 1)
            return ps_box[box]

        def give(ins, key):
            ins.then_inc(box_free[boxes[key][0]], 1)

        def given(eng, key):
            box, use = boxes[key]
            eng.wait_ge(box_free[box], use + 1)

        def weight(pe, key):
            slot, count, _ = weights[key]
            pe.wait_ge(w_landed[slot], count)
            return w_slots[:, slot, 0:DC * WC].rearrange("p (c n) -> p c n", c=DC)

        def weight_keys(key):
            return w_slots[:, weights[key][0], DC * WC:DC * WC + 2 * P].rearrange("p (j d) -> p j d", j=2)

        def load_weight(sp, key, src, col, extra=None):
            slot, _, before = weights[key]
            if key[0] == "wmod" and key[2] >= NW:
                sp.wait_ge(S("wmod_read", key[1]), key[2] - NW + 1)
            elif before is not None:
                box, use = boxes[before[1]]
                sp.wait_ge(box_ready[box], use + 1)
            view = w_slots[:, slot, 0:DC * WC].rearrange("p (c n) -> p c n", c=DC)
            sp.dma_start(view, src.rearrange("(c p) n -> p c n", p=P)[:, :, col:col + WC]).then_inc(w_landed[slot], 16)
            if extra is not None:
                sp.dma_start(weight_keys(key), extra).then_inc(w_landed[slot], 16)

        def tokens(g):
            return P * len(BLOCKS[g])

        def ht(g):
            return HT[:, 0:8 * tokens(g)].rearrange("p (c t) -> p c t", c=8)

        def cat(g):
            return CAT[:, 0:8 * tokens(g)].rearrange("p (c t) -> p c t", c=8)

        def seg_of(l, g, b):
            return 5 * l + BLOCKS[g][b]

        def conv_u(g):
            t = tokens(g)
            return AR[:, 0:4 * (t + 2 * PAD)].rearrange("p (c t) -> p c t", c=4)

        Q_AT, K_AT, V_AT, MU_AT, RS_AT, CW_AT = 2168, 4216, 5496, 6136, 6648, 7160

        def q_t(g):
            return AR[:, Q_AT:Q_AT + 4 * tokens(g)].rearrange("p (c t) -> p c t", c=4)

        def n_keys(g):
            return tokens(g) + (P if g == SMP else 0)

        def k_t(g):
            return AR[:, K_AT:K_AT + 2 * n_keys(g)].rearrange("p (v t) -> p v t", v=2)

        v_t = AR[:, V_AT:V_AT + 640].rearrange("p (b n) -> p b n", b=5)
        cw = AR[:, CW_AT:CW_AT + 4 * CW_ROWS].rearrange("p (c r) -> p c r", c=4)
        raw = CAT[:, 0:768]
        nrm = CAT[:, 768:768 + QK]
        rot = CAT[:, 1408:1408 + QK]
        kdup = CAT[:, 2048:2304]
        gain = CAT[:, 2304:2304 + QK]
        rt1 = CAT[:, 2944:3264]
        rt2 = CAT[:, 3264:3584]
        cw_raw = CAT[0:CW_ROWS, 3584:4096]
        prob = HT[:, 2048:2688]
        prob_t = HT[:, 2688:3328].rearrange("p (b n) -> p b n", b=5)
        o_tok = HT[:, 3328:3840]

        def h_tile(b):
            return CAT[:, (b % 2) * D:(b % 2) * D + D]

        def small(b):
            return AR[:, MU_AT + 512 * (b % 2):MU_AT + 512 * (b % 2) + 512]

        def conv_out(g):
            return HT[:, 0:4 * tokens(g)].rearrange("p (c t) -> p c t", c=4)

        def conv_sq(g):
            return AR[:, 0:4 * tokens(g)].rearrange("p (c t) -> p c t", c=4)

        def f_t(g):
            return AR[:, 0:4 * tokens(g)].rearrange("p (c t) -> p c t", c=4)

        def y_tok(g):
            n = len(BLOCKS[g])
            return AR[:, 2048:2048 + n * 1024].rearrange("p (b g n) -> p b g n", b=n, g=4)

        gc_sb = AR[:, 6144:6656]
        s_pad = AR[:, 6656:7170]
        cw_odd = AR[:, 7170:7182].rearrange("p (c r) -> p c r", c=4)
        def dft_t(g):
            n = len(BLOCKS[g])
            return HT[:, 0:2 * n * tokens(g)].rearrange("p (s b t) -> p s b t", s=2, b=n)

        def q_sb(g, j):
            return AR[:, j * 512:j * 512 + tokens(g)]

        ky_sb = AR[:, 1024:1280].rearrange("p (j k) -> p j k", j=2)

        def stage(g, j):
            n = len(BLOCKS[g])
            return AR[:, 1280 + 1024 * j:1280 + 1024 * j + n * 256].rearrange("p (b j k) -> p b j k", b=n, j=2)

        cond_raw = AR[0:16, 0:P]
        cond_t = AR[:, 128:144]
        mod_sb = AR[:, 144:240]
        mod_row = AR[0:96, 256:384]
        mod_bias = AR[0:96, 384:512]
        mod_gain = AR[0:96, 512:640]
        mod_mask = AR[0:96, 640:641]

        block = ctx.enter_context(nc.Block())

        @block.sync
        def _(sp):
            per_seg = {(topk_done, ""): (8, 3), (h_ready, ""): (1, 1), (x_new, ""): (1, 0), (y_new, ""): (1, -5), (x_stored, ""): (16, 0)}
            for dst, src in ((ident, "ident"), (dft_ch, "dft_ch"), (iota16, "iota16"), (rope, "rope")):
                sp.dma_start(dst[:], T[src]).then_inc(const_in, 16)

            def mod(l):
                sp.dma_start(cond_raw[0:8, :], T["c_ctx"].rearrange("(k p) -> k p", p=P)).then_inc(S("mod_in", l), 16)
                sp.dma_start(cond_raw[8:16, :], T["c"][0].rearrange("(k p) -> k p", p=P)).then_inc(S("mod_in", l), 16)
                for g in range(2):
                    sp.dma_start(mod_bias[48 * g:48 * g + 48, :], T["b_mod"][l].rearrange("(k p) -> k p", p=P)).then_inc(S("mod_in", l), 16)
                sp.dma_start(mod_mask, T["scale_rows"]).then_inc(S("mod_in", l), 16)
                sp.wait_ge(S("gain_one", l), 1)
                for g in range(2):
                    for j, name in ((1, "norm_mix_g"), (4, "norm_ffn_g")):
                        sp.dma_start(mod_gain[48 * g + 8 * j:48 * g + 8 * j + 8, :],
                                     T[name][l].rearrange("(k p) -> k p", p=P)).then_inc(S("mod_in", l), 16)
                for s in range(24):
                    load_weight(sp, ("wmod", l, s), T["w_mod"][l], s * WC)
                sp.wait_ge(S("mod_row", l), 1)
                sp.dma_start(modrow[l].rearrange("g m (k p) -> (g m k) p", p=P), mod_row).then_inc(S("mod_out", l), 16)
                sp.wait_ge(S("mod_out", l), 16)

            def load_bc(l, g, m, slot, name):
                sp.dma_start(BC[:, slot, :], modrow[l, g, m].partition_broadcast(P)).then_inc(S(name, l, g), 16)

            def mix_in(l, g):
                for b in range(len(BLOCKS[g])):
                    if l == 1:
                        src = xb[BLOCKS[g][b]]
                    else:
                        src = T["x_prompt" if g == CTX else "x_sample"][0, b * P:(b + 1) * P, :]
                    sp.dma_start(XM[:, b, :], src).then_inc(S("xm_in", l, g), 16)
                load_bc(l, g, 1, 0, "bc_in")
                load_bc(l, g, 0, 1, "bc_in")
                if l == 0:
                    sp.dma_start(cw_raw[0:CONVK, :], T["conv_dw_w"][0]).then_inc(S("cw_in", l, g), 16)
                    for j, name in enumerate(("conv_dw_b", "conv_ln_g", "conv_ln_b")):
                        sp.dma_start(cw_raw[CONVK + j:CONVK + j + 1, :], T[name]).then_inc(S("cw_in", l, g), 16)
                    for h in range(10):
                        sp.dma_start(gain[:, HD * h:HD * (h + 1)],
                                     T["q_norm_g" if h < 8 else "k_norm_g"][0].partition_broadcast(P)).then_inc(S("gain_in", g), 16)
                else:
                    sp.dma_start(cw_raw[0:3, :], T["short_conv_w"][0]).then_inc(S("cw_in", l, g), 16)

            def even_in(g):
                w = T["w_in_even"][0]
                for s in (0, 2, 1, 3, 4, 5, 6):
                    load_weight(sp, ("win", 0, g, s), w, s * WC)
                    if s == 3 and g == SMP:
                        box, use = boxes[("hT", 0, g, 3)]
                        sp.wait_ge(box_ready[box], use + 1)
                        sp.dma_start(raw[:, 512:640], T["cache_k"][0, 0].rearrange("t v d -> t (v d)")).then_inc(S("cache_in"), 16)
                        sp.dma_start(v_t[:, 0, :], T["cache_v"][0, 0].rearrange("t v d -> t (v d)")).then_inc(S("cache_in"), 16)

            def kv_out():
                sp.wait_ge(S("rot", CTX), 1)
                sp.dma_start(new_k[0, 0].rearrange("t v d -> t (v d)"), rot[:, 512:640]).then_inc(S("kv_out"), 16)
                sp.dma_start(new_v[0, 0].rearrange("t v d -> t (v d)"), v_t[:, 0, :]).then_inc(S("kv_out"), 16)
                sp.wait_ge(S("kv_out"), 32)

            def odd_in(g):
                for s in (0, 1, 2, 4, 6, 3, 5, 7):
                    load_weight(sp, ("win", 1, g, s), T["w_in_odd"][0], s * WC)
                box, use = boxes[("gb", g, 3)]
                sp.wait_ge(box_ready[box], use + 1)
                sp.dma_start(dft_t(g), T["dft_ctx" if g == CTX else "dft_smp"]).then_inc(S("dft_in", g), 16)

            def out_in(l, g):
                nb = len(BLOCKS[g])
                sp.wait_ge(S("h_tok", l, g), nb)
                load_bc(l, g, 2, 0, "bc_gate")
                for s in range(4):
                    load_weight(sp, ("wout", l, g, s), T["w_out_even" if l == 0 else "w_out_odd"][0], s * WC)
                sp.wait_ge(S("x_mixed", l, g), 1)
                load_bc(l, g, 4, 0, "bc_ffn")
                load_bc(l, g, 3, 1, "bc_ffn")
                for b in range(nb):
                    sp.dma_start(xa[seg_of(l, g, b)], XM[:, b, :]).then_inc(S("xa_out", l, g), 16)

            def store_scores(l, g, h):
                given(sp, ("sc", l, g, 2 * h + 1))
                for b in range(len(BLOCKS[g])):
                    sp.dma_start(sc[8 * seg_of(l, g, b) + h].rearrange("p j k -> p (j k)"),
                                 stage(g, h % 2)[:, b].rearrange("p j k -> p (j k)")).then_inc(S("stage_out", l, g, h % 2), 16)

            def prep(l, g, lo, hi):
                nb = len(BLOCKS[g])
                for s in range(lo, hi):
                    load_weight(sp, ("wq", l, g, s), T["peer_wq"][l], s * WC,
                                extra=T["peer_keys"][l].rearrange("h j k d -> k (h j) d")[:, 2 * s:2 * s + 2, :])
                    if s == 2:
                        for b in range(nb):
                            sp.wait_ge(S("h2_tok", l, g), b + 1)
                            sp.dma_start(hs[seg_of(l, g, b)], XM[:, b, :]).then_inc(S("hs_out", l, g), 16)
                    if s >= 3:
                        store_scores(l, g, s - 3)
                if hi == 8:
                    for h in (5, 6, 7):
                        store_scores(l, g, h)
                    for par in range(2):
                        sp.wait_ge(S("stage_out", l, g, par), 16 * nb * 4)
                    sp.wait_ge(S("hs_out", l, g), 16 * nb)
                    sp.wait_ge(S("xa_out", l, g), 16 * nb)

            def load_s(seg, h):
                i = seg * 8 + h
                wait(sp, topk_done, i - 1)
                sp.dma_start(s_buf[:, h % 2], sc[index(i)]).then_inc(s_landed[h % 2], 16)

            def load_h(seg):
                wait(sp, h_ready, seg)
                sp.dma_start(h_next[:, :], hs[index(seg)]).then_inc(h_landed, 16)

            def load_seg(seg, l, g):
                sp.dma_start(x_seg[:, :], xa[index(seg)]).then_inc(seg_landed, 16)
                sp.dma_start(g_seg[:, :], modrow[l, g, 5].partition_broadcast(P)).then_inc(seg_landed, 16)

            def store_seg(seg, l):
                if l == 0:
                    wait(sp, x_new, seg + 1)
                    sp.dma_start(xb[index(seg)], x_seg[:, :]).then_inc(x_stored, 16)
                else:
                    wait(sp, y_new, seg - 4)
                    dst = y_prompt[0] if isinstance(seg, int) and seg == 5 else y_sample[0].rearrange("(b p) d -> b p d", p=P)[index(seg - 6)]
                    sp.dma_start(dst, t_seg[:, :]).then_inc(x_stored, 16)
                wait(sp, x_stored, 16 * (seg + 1))

            def segment(seg, l, g, l_before):
                load_h(seg + 1)
                store_seg(seg - 1, l_before)
                load_seg(seg, l, g)
                for h in range(HEADS):
                    load_s(seg + (h + 4) // 8, (h + 4) % 8)

            mod(0)
            mix_in(0, CTX)
            even_in(CTX)
            kv_out()
            out_in(0, CTX)
            prep(0, CTX, 0, 8)
            load_s(0, 0)
            load_s(0, 1)
            load_h(0)
            load_s(0, 2)
            load_s(0, 3)
            load_seg(0, 0, CTX)
            mix_in(0, SMP)
            even_in(SMP)
            for h in range(4, 8):
                load_s(0, h)
            out_in(0, SMP)
            prep(0, SMP, 0, 8)
            load_h(1)
            for h in range(4):
                load_s(1, h)
            store_seg(0, 0)
            load_seg(1, 0, SMP)
            load_h(2)
            mod(1)
            load_s(1, 4)
            mix_in(1, CTX)
            load_s(1, 5)
            odd_in(CTX)
            load_s(1, 6)
            load_s(1, 7)
            out_in(1, CTX)
            prep(1, CTX, 0, 8)
            for h in range(4):
                load_s(2, h)
            with Segments(sp, 2, 4, per_seg) as seg:
                segment(seg, 0, SMP, 0)
            segment(4, 0, SMP, 0)
            store_seg(4, 0)
            load_seg(5, 1, CTX)
            mix_in(1, SMP)
            load_s(5, 4)
            odd_in(SMP)
            for h in range(5, 8):
                load_s(5, h)
            out_in(1, SMP)
            prep(1, SMP, 0, 8)
            sp.dma_start(BC[:, 0, :], T["final_norm_g"].partition_broadcast(P)).then_inc(fg_landed, 16)
            load_h(6)
            for h in range(4):
                load_s(6, h)
            segment(6, 1, SMP, 1)
            with Segments(sp, 7, 9, per_seg) as seg:
                segment(seg, 1, SMP, 1)
            store_seg(8, 1)
            load_seg(9, 1, SMP)
            for h in range(4, 8):
                load_s(9, h)
            store_seg(9, 1)

        @block.gpsimd
        def _(pool):
            per_seg = {(dots_done, ""): (128, 1 - NU), (vsum_done, ""): (128, 1 - NV - TOPK), (topk_done, ""): (8, 1)}
            u_rows = T["peer_u"].rearrange("l e d -> (l e) d")
            v_rows = T["peer_v"].rearrange("l e d -> (l e) d")

            def gather_u(i, h, k):
                wait(pool, dots_done, 16 * i + k - NU + 1)
                pool.indirect_dma_start(out=u_ring[:, k % NU, :], out_offset=None, in_=u_rows,
                                        in_offset=bass.IndirectOffsetOnAxis(ap=idx[:, h % 4, k:k + 1], axis=0)
                                        ).then_inc(u_landed[k % NU], 16)

            def gather_v(i, h, k):
                wait(pool, vsum_done, 16 * i + k - NV + 1)
                pool.indirect_dma_start(out=v_ring[:, k % NV, :], out_offset=None, in_=v_rows,
                                        in_offset=bass.IndirectOffsetOnAxis(ap=idx[:, h % 4, k:k + 1], axis=0)
                                        ).then_inc(v_landed[k % NV], 16)

            def step(seg, h, first=False):
                i = seg * 8 + h
                wait(pool, topk_done, i + 1)
                for k in range(TOPK):
                    gather_u(i, h, k)
                    if not first:
                        gather_v(i - 1, h - 1, k)

            for i in range(16):
                step(i // 8, i % 8, first=i == 0)
            with Segments(pool, 2, 4, per_seg) as seg:
                for h in range(HEADS):
                    step(seg, h)
            for i in range(32, 48):
                step(i // 8, i % 8)
            with Segments(pool, 6, 9, per_seg) as seg:
                for h in range(HEADS):
                    step(seg, h)
            for h in range(HEADS):
                step(9, h)
            for k in range(TOPK):
                gather_v(79, 7, k)

        @block.tensor
        def _(pe):
            per_seg = {(acc_free, ""): (1, 0), (diag_done, ""): (128, 1), **{(s, ""): (256, 16) for s in v_landed}}
            pe.wait_ge(const_in, 64)

            def step(seg, h, lo=0, hi=TOPK):
                i = seg * 8 + h
                for k in range(lo, hi):
                    if h == 0 and k == 0:
                        wait(pe, acc_free, seg)
                    wait(pe, diag_done, 16 * i + k + 1)
                    wait(pe, v_landed[k % NV], 32 * i + 16 * (k // NV) + 16)
                    for half in range(2):
                        last = nc.tensor.matmul(ps_v[:, 512 * half:512 * half + 512], diag[:, k % NDIAG, :],
                                                v_ring[:, k % NV, 512 * half:512 * half + 512],
                                                start=(h == 0 and k == 0), stop=(h == 7 and k == TOPK - 1))
                    last.then_inc(vsum_done, 1)

            def mod(l):
                pe.wait_ge(S("mod_in", l), 16 * 9)
                box = fill(pe, ("condT", l))
                filled(nc.tensor.transpose(box[:, 0:16], cond_raw, ident[0:16, 0:16]), ("condT", l))
                given(pe, ("condT", l))
                box = fill(pe, ("mod", l))
                ct = cond_t.rearrange("p (g c) -> p c g", g=2)
                for s in range(24):
                    w = weight(pe, ("wmod", l, s))
                    for j in range(2):
                        for c in range(DC):
                            last = nc.tensor.matmul(box[:, 2 * (2 * s + j):2 * (2 * s + j) + 2], w[:, c, j * P:(j + 1) * P],
                                                    ct[:, c, :], start=(c == 0), stop=(c == DC - 1))
                    if s < 24 - NW:
                        last.then_inc(S("wmod_read", l), 1)
                filled(last, ("mod", l))
                given(pe, ("mod", l))
                box = fill(pe, ("modT", l))
                filled(nc.tensor.transpose(box[0:96, 0:P], mod_sb, ident[:, :]), ("modT", l))

            def cw_turn(l, g):
                rows = CW_ROWS if l == 0 else 3
                pe.wait_ge(S("cw_in", l, g), 16 * (4 if l == 0 else 1))
                box = fill(pe, ("cwT", l, g))
                for c in range(4):
                    last = nc.tensor.transpose(box[:, c * rows:(c + 1) * rows], cw_raw[0:rows, c * P:(c + 1) * P],
                                               ident[0:rows, 0:rows])
                filled(last, ("cwT", l, g))

            def turn_h(l, g, name, ready):
                for b in range(len(BLOCKS[g])):
                    pe.wait_ge(S(ready, l, g), b + 1)
                    box = fill(pe, (name, l, g, b))
                    src = h_tile(b) if name == "hT" else XM[:, b, :]
                    for c in range(DC):
                        last = nc.tensor.transpose(box[:, c * P:(c + 1) * P], src[:, c * P:(c + 1) * P], ident[:, :])
                    filled(last, (name, l, g, b))

            def proj_t(out, w, col, g):
                h = ht(g)
                for c in range(DC):
                    last = nc.tensor.matmul(out, w[:, c, col:col + P], h[:, c, :], start=(c == 0), stop=(c == DC - 1))
                return last

            def even_a(g):
                t, nb = tokens(g), len(BLOCKS[g])
                given(pe, ("hT", 0, g, nb - 1))
                for c in range(4):
                    wv = weight(pe, ("win", 0, g, c // 2))
                    wg = weight(pe, ("win", 0, g, 2 + c // 2))
                    box = fill(pe, ("vg", g, c))
                    proj_t(box[:, 512:512 + t], wg, (c % 2) * P, g)
                    filled(proj_t(box[:, 0:t], wv, (c % 2) * P, g), ("vg", g, c))

            def even_qkv(g):
                nb = len(BLOCKS[g])
                h = ht(g)
                if g == SMP:
                    pe.wait_ge(S("cache_dup"), 1)
                    box = fill(pe, ("ckT", g))
                    for v in range(2):
                        last = nc.tensor.transpose(box[:, v * P:(v + 1) * P], kdup[:, v * P:(v + 1) * P], ident[:, :])
                    filled(last, ("ckT", g))
                for b in range(nb):
                    box = fill(pe, ("qkv", g, b))
                    for s in range(3):
                        w = weight(pe, ("win", 0, g, 4 + s))
                        for c in range(DC):
                            last = nc.tensor.matmul(box[:, s * WC:(s + 1) * WC], h[:, c, b * P:(b + 1) * P], w[:, c, :],
                                                    start=(c == 0), stop=(c == DC - 1))
                    filled(last, ("qkv", g, b))
                    pe.wait_ge(S("rot", g), b + 1)
                    box = fill(pe, ("qkT", g, b))
                    for c in range(4):
                        nc.tensor.transpose(box[:, c * P:(c + 1) * P], rot[:, c * P:(c + 1) * P], ident[:, :])
                    for v in range(2):
                        last = nc.tensor.transpose(box[:, 512 + v * P:512 + (v + 1) * P], kdup[:, v * P:(v + 1) * P], ident[:, :])
                    filled(last, ("qkT", g, b))

            def attend(g, b):
                nk = n_keys(g)
                q, k = q_t(g), k_t(g)
                given(pe, ("qkT", g, len(BLOCKS[g]) - 1))
                for h in range(HEADS):
                    lo = HD * (h % 2)
                    box = fill(pe, ("S", g, b, h))
                    for at in range(0, nk, 512):
                        to = min(nk, at + 512)
                        last = nc.tensor.matmul(box[:, at:to], q[lo:lo + HD, h // 2, b * P:(b + 1) * P],
                                                k[lo:lo + HD, h // 4, at:to], start=True, stop=True)
                    filled(last, ("S", g, b, h))
                    given(pe, ("S", g, b, h))
                    box = fill(pe, ("PT", g, b, h))
                    for kb in range(nk // P):
                        last = nc.tensor.transpose(box[:, kb * P:(kb + 1) * P], prob[:, kb * P:(kb + 1) * P], ident[:, :])
                    filled(last, ("PT", g, b, h))
                    given(pe, ("PT", g, b, h))
                    box = fill(pe, ("O", g, b, h))
                    for kb in range(nk // P):
                        last = nc.tensor.matmul(box[:, 0:HD], prob_t[:, kb, :], v_t[:, kb, HD * (h // 4):HD * (h // 4) + HD],
                                                start=(kb == 0), stop=(kb == nk // P - 1))
                    filled(last, ("O", g, b, h))
                given(pe, ("O", g, b, 7))
                box = fill(pe, ("oT", g, b))
                for c in range(4):
                    last = nc.tensor.transpose(box[:, c * P:(c + 1) * P], o_tok[:, c * P:(c + 1) * P], ident[:, :])
                filled(last, ("oT", g, b))

            def conv_norm(g):
                t = tokens(g)
                pe.wait_ge(S("conv", g), 4 * CONVK)
                for key, src, ready in (("mean", conv_out(g), None), ("var", conv_sq(g), "conv_sq")):
                    if ready:
                        pe.wait_ge(S(ready, g), 1)
                    box = fill(pe, (key, g))
                    for c in range(4):
                        last = nc.tensor.matmul(box[:, 0:t], ones[:, :], src[:, c, :], start=(c == 0), stop=(c == 3))
                    filled(last, (key, g))

            def odd_a(g):
                t, nb = tokens(g), len(BLOCKS[g])
                given(pe, ("hT", 1, g, nb - 1))
                for c in range(4):
                    w = weight(pe, ("win", 1, g, c // 2))
                    box = fill(pe, ("fT", g, c))
                    filled(proj_t(box[:, 0:t], w, (c % 2) * P, g), ("fT", g, c))
                for c in range(4):
                    box = fill(pe, ("cv", g, c))
                    proj_t(box[:, 0:t], weight(pe, ("win", 1, g, 4 + c // 2)), (c % 2) * P, g)
                    last = proj_t(box[:, 512:512 + t], weight(pe, ("win", 1, g, 6 + c // 2)), (c % 2) * P, g)
                    filled(last, ("cv", g, c))
                    box = fill(pe, ("gb", g, c))
                    filled(proj_t(box[:, 0:t], weight(pe, ("win", 1, g, 2 + c // 2)), (c % 2) * P, g), ("gb", g, c))

            def odd_fft(g):
                t, nb = tokens(g), len(BLOCKS[g])
                f, y = f_t(g), y_tok(g)
                given(pe, ("fT", g, 3))
                for b in range(nb):
                    box = fill(pe, ("Y", g, b))
                    for c in range(4):
                        last = nc.tensor.matmul(box[:, c * 256:(c + 1) * 256], f[:, c, b * P:(b + 1) * P], dft_ch[:, :],
                                                start=True, stop=True)
                    filled(last, ("Y", g, b))
                given(pe, ("Y", g, nb - 1))
                pe.wait_ge(S("dft_in", g), 16)
                d = dft_t(g)
                for c in range(4):
                    box = fill(pe, ("ffT", g, c))
                    for b in range(nb):
                        for s in range(2):
                            last = nc.tensor.matmul(box[:, 0:t], y[:, b, c, s * P:(s + 1) * P], d[:, s, b, :],
                                                    start=(b == 0 and s == 0), stop=(b == nb - 1 and s == 1))
                    filled(last, ("ffT", g, c))

            def mix_out(l, g):
                nb = len(BLOCKS[g])
                x = cat(g)
                if l == 0:
                    pe.wait_ge(S("cat_a", g), 4)
                    given(pe, ("oT", g, nb - 1))
                else:
                    given(pe, ("gb", g, 3))
                    given(pe, ("ffT", g, 3))
                for s in range(4):
                    w = weight(pe, ("wout", l, g, s))
                    for b in range(nb):
                        box = fill(pe, ("out", l, g, s, b))
                        for c in range(8):
                            last = nc.tensor.matmul(box[:, 0:WC], x[:, c, b * P:(b + 1) * P], w[:, c, :],
                                                    start=(c == 0), stop=(c == 7))
                        filled(last, ("out", l, g, s, b))

            def scores(l, g, lo=0, hi=8):
                nb = len(BLOCKS[g])
                t = tokens(g)
                given(pe, ("h2T", l, g, nb - 1))
                for s in range(lo, hi):
                    w = weight(pe, ("wq", l, g, s))
                    kr = weight_keys(("wq", l, g, s))
                    box = fill(pe, ("kyT", l, g, s))
                    for j in range(2):
                        last = nc.tensor.transpose(box[:, j * P:(j + 1) * P], kr[:, j, :], ident[:, :])
                    filled(last, ("kyT", l, g, s))
                    for j in range(2):
                        n = 2 * s + j
                        box = fill(pe, ("q", l, g, n))
                        filled(proj_t(box[:, 0:t], w, j * P, g), ("q", l, g, n))
                        given(pe, ("q", l, g, n))
                        given(pe, ("kyT", l, g, s))
                        box = fill(pe, ("sc", l, g, n))
                        for b in range(nb):
                            last = nc.tensor.matmul(box[:, b * P:(b + 1) * P], q_sb(g, j)[:, b * P:(b + 1) * P], ky_sb[:, j, :],
                                                    start=True, stop=True)
                        filled(last, ("sc", l, g, n))

            mod(0)
            cw_turn(0, CTX)
            turn_h(0, CTX, "hT", "h_tok")
            even_a(CTX)
            even_qkv(CTX)
            attend(CTX, 0)
            conv_norm(CTX)
            mix_out(0, CTX)
            turn_h(0, CTX, "h2T", "h2_tok")
            scores(0, CTX)
            cw_turn(0, SMP)
            turn_h(0, SMP, "hT", "h_tok")
            step(0, 0)
            even_a(SMP)
            step(0, 1)
            even_qkv(SMP)
            for b in range(4):
                step(0, 2 + b)
                attend(SMP, b)
            conv_norm(SMP)
            step(0, 6)
            mix_out(0, SMP)
            turn_h(0, SMP, "h2T", "h2_tok")
            scores(0, SMP)
            step(0, 7)
            step(1, 0)
            mod(1)
            step(1, 1)
            cw_turn(1, CTX)
            turn_h(1, CTX, "hT", "h_tok")
            odd_a(CTX)
            step(1, 2)
            odd_fft(CTX)
            step(1, 3)
            mix_out(1, CTX)
            step(1, 4)
            turn_h(1, CTX, "h2T", "h2_tok")
            scores(1, CTX)
            for h in range(5, 8):
                step(1, h)
            with Segments(pe, 2, 4, per_seg) as seg:
                for h in range(HEADS):
                    step(seg, h)
            for h in range(HEADS):
                step(4, h)
            step(5, 0)
            cw_turn(1, SMP)
            turn_h(1, SMP, "hT", "h_tok")
            step(5, 1)
            odd_a(SMP)
            step(5, 2)
            odd_fft(SMP)
            step(5, 3)
            mix_out(1, SMP)
            step(5, 4)
            turn_h(1, SMP, "h2T", "h2_tok")
            step(5, 5)
            scores(1, SMP)
            step(5, 6)
            step(5, 7)
            with Segments(pe, 6, 9, per_seg) as seg:
                for h in range(HEADS):
                    step(seg, h)
            for h in range(HEADS):
                step(9, h)

        @block.scalar
        def _(act):
            per_seg = {(w_done, "diags"): (8, 0), (w_done, "gelu"): (8, -1), (w_done, "exps"): (8, -1),
                      (vsum_done, ""): (128, 1 - NDIAG - TOPK), (dots_done, ""): (128, 16), (negmax_done, ""): (8, 3),
                      (h_landed, ""): (16, 32), (x_new, ""): (1, 0)}
            chain = Chain(act, act_chain)
            act.wait_ge(const_in, 64)
            act.wait_ge(S("ones_set"), 1)

            def diags(seg, h, lo=0, hi=TOPK):
                i = seg * 8 + h
                for k in range(lo, hi):
                    if k == 0:
                        wait(act, w_done, i + 1, "diags")
                    wait(act, vsum_done, 16 * i + k - NDIAG + 1)
                    nc.scalar.activation(diag[:, k % NDIAG, :], ident[:, :], ACT.Copy,
                                         scale=w_v[:, h % 2, k:k + 1]).then_inc(diag_done, 1)

            def gelu(seg, h):
                i = seg * 8 + h
                wait(act, w_done, i - 1, "gelu")
                wait(act, dots_done, 16 * i + 16)
                nc.scalar.activation(gelu_v[:, h % 2, :], act_v[:, h % 2, :], ACT.Gelu_apprx_tanh).then_inc(gelu_done, 1)

            def exps(seg, h):
                i = seg * 8 + h
                wait(act, negmax_done, i + 1)
                wait(act, w_done, i - 3, "exps")
                nc.scalar.activation(ex[:, h % 4, :], fv[:, h % 2, :], ACT.Exp, bias=neg_max[:, h % 2:h % 2 + 1],
                                     accum_out=ex_sum[:, h % 4:h % 4 + 1]).then_inc(exp_done, 1)

            def take_h(seg):
                wait(act, h_landed, 16 * seg + 16)
                nc.scalar.activation(h_cur[:, :], h_next[:, :], ACT.Copy).then_inc(h_ready, 1)

            def seg_square(seg):
                wait(act, x_new, seg + 1)
                chain(nc.scalar.activation(t_seg[:, :], x_seg[:, :], ACT.Square, accum_out=seg_st[:, 0:1]))
                nc.scalar.activation(seg_st[:, 1:2], seg_st[:, 0:1], ACT.Sqrt, bias=eps[:, 0:1], scale=1.0 / D).then_inc(ss_done, 1)

            def step(seg, h, after=None, ends=None, topk=True):
                if h:
                    diags(seg, h - 1)
                elif after is None:
                    diags(seg - 1, 7)
                gelu(seg, h)
                if ends is not None:
                    seg_square(ends)
                if h == 7 and topk:
                    take_h(seg + 1)
                if topk:
                    exps(seg + (h + 2) // 8, (h + 2) % 8)

            def mod(l):
                act.activation(cond_t, take(act, ("condT", l))[:, 0:16], ACT.Silu).then_inc(box_free[boxes[("condT", l)][0]], 1)
                box = take(act, ("mod", l))
                give(nc.scalar.activation(mod_sb.rearrange("p (g j) -> p g j", g=2), box[:, 0:96].rearrange("p (j g) -> p g j", g=2),
                                          ACT.Copy), ("mod", l))

            def cw_sb(l, g):
                rows = CW_ROWS if l == 0 else 3
                box = take(act, ("cwT", l, g))
                dst = cw if l == 0 else cw_odd
                act.wait_ge(S("xm_in", l, g), 16 * len(BLOCKS[g]))
                give(nc.scalar.activation(dst, box[:, 0:4 * rows].rearrange("p (c r) -> p c r", c=4), ACT.Copy), ("cwT", l, g))

            def norm(l, g, name):
                nb = len(BLOCKS[g])
                at = 0 if name == "hT" else 12
                if name == "hT":
                    act.wait_ge(S("xm_in", l, g), 16 * nb)
                else:
                    act.wait_ge(S("x_mixed", l, g), 1)
                for b in range(nb):
                    if name == "hT" and b >= 2:
                        box, use = boxes[("hT", l, g, b - 2)]
                        act.wait_ge(box_ready[box], use + 1)
                    chain(nc.scalar.activation(h_tile(b), XM[:, b, :], ACT.Square, accum_out=st[:, at + b:at + b + 1]))
                    nc.scalar.activation(st[:, at + 4 + b:at + 5 + b], st[:, at + b:at + b + 1], ACT.Sqrt, bias=eps[:, 0:1],
                                         scale=1.0 / D).then_inc(S("rms", name, l, g), 1)
                    if b >= 1:
                        h_sb(l, g, name, b - 1)
                h_sb(l, g, name, nb - 1)

            def h_sb(l, g, name, b):
                box = take(act, (name, l, g, b))
                give(nc.scalar.activation(ht(g)[:, :, b * P:(b + 1) * P], box[:, :].rearrange("p (c t) -> p c t", c=8), ACT.Copy),
                     (name, l, g, b))

            def even_a(g):
                t = tokens(g)
                for c in range(4):
                    box = take(act, ("vg", g, c))
                    if c >= 2:
                        given(act, ("vg", g, c - 2))
                    nc.scalar.activation(small(c)[:, 0:t], box[:, 512:512 + t], ACT.Sigmoid).then_inc(S("sig", g), 1)

            def even_qkv(g):
                off = 1 if g == SMP else 0
                if g == SMP:
                    box = take(act, ("ckT", g))
                    give(nc.scalar.activation(k_t(g)[:, :, 0:P], box[:, 0:256].rearrange("p (v t) -> p v t", v=2), ACT.Copy), ("ckT", g))
                for b in range(len(BLOCKS[g])):
                    box = take(act, ("qkv", g, b))
                    if b:
                        act.wait_ge(S("rot", g), b)
                    elif g == SMP:
                        act.wait_ge(S("cache_dup"), 1)
                    nc.scalar.activation(raw[:, 0:QK], box[:, 0:QK], ACT.Copy)
                    give(nc.scalar.activation(v_t[:, b + off, :], box[:, QK:QK + P], ACT.Copy), ("qkv", g, b))
                    act.wait_ge(S("qk_ss", g), b + 1)
                    nc.scalar.activation(st[:, 34:44], st[:, 24:34], ACT.Sqrt, bias=eps[:, 0:1], scale=1.0 / HD).then_inc(S("qk_rms", g), 1)
                    box = take(act, ("qkT", g, b))
                    nc.scalar.activation(q_t(g)[:, :, b * P:(b + 1) * P], box[:, 0:512].rearrange("p (c t) -> p c t", c=4), ACT.Copy)
                    give(nc.scalar.activation(k_t(g)[:, :, (b + off) * P:(b + off + 1) * P],
                                              box[:, 512:768].rearrange("p (v t) -> p v t", v=2), ACT.Copy), ("qkT", g, b))

            def attend(g, b):
                nk = n_keys(g)
                for h in range(HEADS):
                    n = b * HEADS + h
                    box = take(act, ("S", g, b, h))
                    act.wait_ge(S("row_max", g), n + 1)
                    if n:
                        bx, use = boxes[("PT", g, (n - 1) // 8, (n - 1) % 8)]
                        act.wait_ge(box_ready[bx], use + 1)
                    give(nc.scalar.activation(prob[:, 0:nk], box[:, 0:nk], ACT.Exp, bias=st[:, 46 + n % 2:47 + n % 2],
                                              scale=HD ** -0.5, accum_out=st[:, 48 + n % 2:49 + n % 2]), ("S", g, b, h))
                    box = take(act, ("PT", g, b, h))
                    if n:
                        bx, use = boxes[("O", g, (n - 1) // 8, (n - 1) % 8)]
                        act.wait_ge(box_ready[bx], use + 1)
                    give(nc.scalar.activation(prob_t[:, 0:nk // P, :], box[:, 0:nk].rearrange("p (b n) -> p b n", n=P), ACT.Copy),
                         ("PT", g, b, h))
                box = take(act, ("oT", g, b))
                give(nc.scalar.activation(cat(g)[:, 4:8, b * P:(b + 1) * P], box[:, 0:512].rearrange("p (c t) -> p c t", c=4), ACT.Copy),
                     ("oT", g, b))

            def conv_norm(g):
                t = tokens(g)
                given(act, ("mean", g))
                nc.scalar.activation(conv_sq(g), conv_out(g), ACT.Square).then_inc(S("conv_sq", g), 1)
                box = take(act, ("var", g))
                give(nc.scalar.activation(small(1)[:, 0:t], box[:, 0:t], ACT.Sqrt, bias=eps[:, 0:1]), ("var", g))
                act.wait_ge(S("conv_unit", g), 1)
                for c in range(4):
                    nc.scalar.activation(cat(g)[:, c, :], conv_out(g)[:, c, :], ACT.Silu, scale=cw[:, c, CONVK + 1:CONVK + 2],
                                         bias=cw[:, c, CONVK + 2:CONVK + 3]).then_inc(S("cat_a", g), 1)

            def odd_a(g):
                t = tokens(g)
                for c in range(4):
                    box = take(act, ("fT", g, c))
                    give(nc.scalar.activation(f_t(g)[:, c, :], box[:, 0:t], ACT.Copy), ("fT", g, c))
                for c in range(4):
                    box = take(act, ("cv", g, c))
                    if c:
                        given(act, ("cv", g, c - 1))
                    nc.scalar.activation(gc_sb[:, 0:t], box[:, 0:t], ACT.Copy).then_inc(S("gc", g), 1)

            def odd_fft(g):
                t = tokens(g)
                for b in range(len(BLOCKS[g])):
                    box = take(act, ("Y", g, b))
                    give(nc.scalar.activation(y_tok(g)[:, b].rearrange("p c n -> p (c n)"), box[:, :], ACT.Copy), ("Y", g, b))
                for c in range(4):
                    box = take(act, ("ffT", g, c))
                    give(nc.scalar.activation(cat(g)[:, c, :], box[:, 0:t], ACT.Copy), ("ffT", g, c))

            def scores(l, g, lo=0, hi=8):
                t, nb = tokens(g), len(BLOCKS[g])
                for s in range(lo, hi):
                    box = take(act, ("kyT", l, g, s))
                    give(nc.scalar.activation(ky_sb, box[:, 0:256].rearrange("p (j k) -> p j k", j=2), ACT.Copy), ("kyT", l, g, s))
                    for j in range(2):
                        n = 2 * s + j
                        box = take(act, ("q", l, g, n))
                        give(nc.scalar.activation(q_sb(g, j), box[:, 0:t], ACT.Copy), ("q", l, g, n))
                        box = take(act, ("sc", l, g, n))
                        if j == 0 and s >= 2:
                            act.wait_ge(S("stage_out", l, g, s % 2), 16 * nb * (s // 2))
                        give(nc.scalar.activation(stage(g, s % 2)[:, :, j, :], box[:, 0:t].rearrange("p (b k) -> p b k", b=nb),
                                                  ACT.Copy), ("sc", l, g, n))

            mod(0)
            cw_sb(0, CTX)
            norm(0, CTX, "hT")
            even_a(CTX)
            even_qkv(CTX)
            attend(CTX, 0)
            conv_norm(CTX)
            norm(0, CTX, "h2T")
            scores(0, CTX)
            exps(0, 0)
            exps(0, 1)
            take_h(0)
            step(0, 0, after=False)
            cw_sb(0, SMP)
            norm(0, SMP, "hT")
            step(0, 1)
            even_a(SMP)
            step(0, 2)
            even_qkv(SMP)
            for b in range(3):
                step(0, 3 + b)
                attend(SMP, b)
            step(0, 6, topk=False)
            attend(SMP, 3)
            conv_norm(SMP)
            step(0, 7, topk=False)
            norm(0, SMP, "h2T")
            scores(0, SMP)
            take_h(1)
            exps(1, 0)
            exps(1, 1)
            step(1, 0)
            step(1, 1)
            mod(1)
            step(1, 2)
            cw_sb(1, CTX)
            norm(1, CTX, "hT")
            odd_a(CTX)
            step(1, 3)
            odd_fft(CTX)
            step(1, 4)
            step(1, 5, topk=False)
            norm(1, CTX, "h2T")
            scores(1, CTX)
            exps(1, 7)
            step(1, 6)
            step(1, 7)
            with Segments(act, 2, 4, per_seg) as seg:
                chain.restart()
                for h in range(HEADS):
                    step(seg, h)
            for h in range(HEADS):
                step(4, h)
            step(5, 0)
            step(5, 1)
            cw_sb(1, SMP)
            norm(1, SMP, "hT")
            step(5, 2)
            odd_a(SMP)
            step(5, 3)
            odd_fft(SMP)
            step(5, 4)
            step(5, 5)
            norm(1, SMP, "h2T")
            step(5, 6, topk=False)
            scores(1, SMP)
            step(5, 7, topk=False)
            take_h(6)
            exps(6, 0)
            exps(6, 1)
            with Segments(act, 6, 9, per_seg) as seg:
                chain.restart()
                for h in range(HEADS):
                    step(seg, h, ends=seg - 1 if h == 0 else None)
            for h in range(6):
                step(9, h, ends=8 if h == 0 else None)
            step(9, 6, topk=False)
            step(9, 7, topk=False)
            diags(9, 7)
            seg_square(9)

        @block.vector
        def _(dve):
            per_seg = {(h_ready, ""): (1, 1), (s_landed[0], ""): (64, 32), (s_landed[1], ""): (64, 32), (exp_done, "topk"): (8, 1),
                      (exp_done, "weigh"): (8, 1), (vsum_done, "end"): (128, 0), (vsum_done, "idx"): (128, -16),
                      (gelu_done, ""): (8, 1), (diag_done, ""): (128, -16), (seg_landed, ""): (32, 0), (acc_free, ""): (1, 0),
                      (ss_done, ""): (1, -5), **{(s, ""): (256, 16) for s in u_landed}}
            chain = Chain(dve, dve_chain)
            nc.vector.memset(eps[:, :], EPS)
            nc.vector.memset(ones[:, :], 1.0 / 512).then_inc(S("ones_set"), 1)
            dve.wait_ge(const_in, 64)

            def dots(seg, h, lo=0, hi=TOPK):
                i = seg * 8 + h
                for k in range(lo, hi):
                    if h == 0 and k == 0:
                        wait(dve, h_ready, seg + 1)
                    wait(dve, u_landed[k % NU], 32 * i + 16 * (k // NU) + 16)
                    nc.vector.tensor_tensor_reduce(u_ring[:, k % NU, :], u_ring[:, k % NU, :], h_cur[:, :], 1.0, 0.0,
                                                   ALU.mult, ALU.add, act_v[:, h % 2, k:k + 1]).then_inc(dots_done, 1)

            def top16(values, indices, src, rep):
                chain(nc.vector.max(values[:, 0:8], src))
                nc.vector.max_index(indices[:, 0:8], values[:, 0:8], src)
                chain(nc.vector.match_replace(rep, values[:, 0:8], src, NEG))
                chain(nc.vector.max(values[:, 8:16], rep))
                chain(nc.vector.max_index(indices[:, 8:16], values[:, 8:16], rep))

            def topk(seg, h, l):
                i = seg * 8 + h
                wait(dve, s_landed[h % 2], 64 * seg + 16 * (h // 2) + 16)
                wait(dve, exp_done, i - 1, "topk")
                for j in range(2):
                    top16(sv[:, j, :], si[:, j, :], s_buf[:, h % 2, j, :], s_rep[:, j, :])
                chain(nc.vector.tensor_tensor(cand[:, :, :], sv[:, 0, :].unsqueeze(2).to_broadcast([P, 16, 16]),
                                              sv[:, 1, :].unsqueeze(1).to_broadcast([P, 16, 16]), ALU.add))
                flat = cand[:, :, :].rearrange("p a b -> p (a b)")
                top16(fv[:, h % 2, :], fi[:, :], flat, cand_rep)
                nc.vector.tensor_scalar(neg_max[:, h % 2:h % 2 + 1], fv[:, h % 2, 0:1], -1.0, None, ALU.mult).then_inc(negmax_done, 1)
                nc.vector.tensor_scalar(ab[:, 0, :], fi[:, :], 4, None, ALU.logical_shift_right)
                chain(nc.vector.tensor_scalar(ab[:, 1, :], fi[:, :], 15, None, ALU.bitwise_and))
                nc.vector.tensor_copy(sif[:, :, :], si[:, :, :])
                chain(nc.vector.tensor_copy(abf[:, :, :], ab[:, :, :]))
                for j in range(2):
                    last = nc.vector.tensor_tensor(onehot[:, j], abf[:, j, :].unsqueeze(2).to_broadcast([P, 16, 16]),
                                                   iota16[:, :].unsqueeze(1).to_broadcast([P, 16, 16]), ALU.is_equal)
                chain(last)
                for j in range(2):
                    last = nc.vector.tensor_tensor(onehot[:, j], onehot[:, j],
                                                   sif[:, j, :].unsqueeze(1).to_broadcast([P, 16, 16]), ALU.mult)
                chain(last)
                chain(nc.vector.tensor_reduce(e01[:, :, :], onehot[:, :, :, :], AX, ALU.add))
                chain(nc.vector.scalar_tensor_tensor(e01[:, 0, :], e01[:, 0, :], float(KEYS), e01[:, 1, :], ALU.mult, ALU.add))
                wait(dve, vsum_done, 16 * (i - 3), "idx")
                nc.vector.tensor_scalar(idx[:, h % 4, :], e01[:, 0, :], float(l * EXPERTS), None, ALU.add).then_inc(topk_done, 1)

            def weigh(seg, h):
                i = seg * 8 + h
                wait(dve, exp_done, i + 1, "weigh")
                chain(nc.vector.reciprocal(ex_rec[:, h % 4:h % 4 + 1], ex_sum[:, h % 4:h % 4 + 1]))
                wait(dve, gelu_done, i + 1)
                wait(dve, diag_done, 16 * (i - 1))
                nc.vector.scalar_tensor_tensor(w_v[:, h % 2, :], gelu_v[:, h % 2, :], ex_rec[:, h % 4:h % 4 + 1], ex[:, h % 4, :],
                                               ALU.mult, ALU.mult).then_inc(w_done, 1)

            def seg_end(seg, l):
                wait(dve, vsum_done, 128 * seg + 128, "end")
                wait(dve, seg_landed, 32 * seg + 32)
                nc.vector.tensor_tensor(t_seg[:, :], ps_v[:, :], g_seg[:, :], ALU.mult).then_inc(acc_free, 1)
                wait(dve, acc_free, seg + 1)
                nc.vector.tensor_tensor(x_seg[:, :], x_seg[:, :], t_seg[:, :], ALU.add).then_inc(x_new, 1)
                if l == 1:
                    dve.wait_ge(fg_landed, 16)
                    wait(dve, ss_done, seg - 4)
                    chain(nc.vector.reciprocal(seg_st[:, 2:3], seg_st[:, 1:2]))
                    nc.vector.scalar_tensor_tensor(t_seg[:, :], x_seg[:, :], seg_st[:, 2:3], BC[:, 0, :], ALU.mult,
                                                   ALU.mult).then_inc(y_new, 1)

            def step(seg, h, l, ends=None, l_ends=0, nxt=True):
                dots(seg, h)
                if ends is not None:
                    seg_end(ends, l_ends)
                if nxt:
                    topk(seg + (h + 2) // 8, (h + 2) % 8, l)
                weigh(seg, h)

            def mod(l):
                nc.vector.memset(mod_gain, 1.0).then_inc(S("gain_one", l), 1)
                dve.wait_ge(S("mod_in", l), 16 * 9)
                box = take(dve, ("modT", l))
                give(nc.vector.tensor_tensor(mod_row, box[0:96, 0:P], mod_bias, ALU.add), ("modT", l))
                given(dve, ("modT", l))
                nc.vector.scalar_tensor_tensor(mod_row, mod_row, mod_mask, mod_gain, ALU.add, ALU.mult).then_inc(S("mod_row", l), 1)

            def norm(l, g, name):
                nb = len(BLOCKS[g])
                at = 0 if name == "hT" else 12
                if name == "hT":
                    dve.wait_ge(S("bc_in", l, g), 32)
                else:
                    dve.wait_ge(S("bc_ffn", l, g), 32)
                    dve.wait_ge(S("xa_out", l, g), 16 * nb)
                for b in range(nb):
                    dve.wait_ge(S("rms", name, l, g), b + 1)
                    r = st[:, at + 8 + b:at + 9 + b]
                    chain(nc.vector.reciprocal(r, st[:, at + 4 + b:at + 5 + b]))
                    dst = h_tile(b) if name == "hT" else XM[:, b, :]
                    chain(nc.vector.scalar_tensor_tensor(dst, XM[:, b, :], r, BC[:, 0, :], ALU.mult, ALU.mult))
                    nc.vector.tensor_tensor(dst, dst, BC[:, 1, :], ALU.add).then_inc(S("h_tok" if name == "hT" else "h2_tok", l, g), 1)

            def even_a(g):
                t = tokens(g)
                u = conv_u(g)
                nc.vector.memset(u[:, :, 0:PAD], 0.0)
                nc.vector.memset(u[:, :, PAD + t:], 0.0)
                for c in range(4):
                    dve.wait_ge(S("sig", g), c + 1)
                    box = take(dve, ("vg", g, c))
                    give(nc.vector.tensor_tensor(u[:, c, PAD:PAD + t], box[:, 0:t], small(c)[:, 0:t], ALU.mult), ("vg", g, c))

            def heads(ap, n=10):
                return ap.rearrange("p (h d) -> p h d", h=n)

            def dup(src, g):
                dst = kdup.rearrange("p (v e d) -> p v e d", v=2, e=2)
                for e in range(2):
                    last = nc.vector.tensor_copy(dst[:, :, e, :], src.rearrange("p (v d) -> p v d", v=2))
                return last

            def even_qkv(g):
                dve.wait_ge(S("gain_in", g), 160)
                if g == SMP:
                    dve.wait_ge(S("cache_in"), 32)
                    dup(raw[:, 512:640], g).then_inc(S("cache_dup"), 1)
                    box, use = boxes[("ckT", g)]
                    dve.wait_ge(box_ready[box], use + 1)
                for b in range(len(BLOCKS[g])):
                    given(dve, ("qkv", g, b))
                    chain(nc.vector.tensor_tensor(nrm, raw[:, 0:QK], raw[:, 0:QK], ALU.mult))
                    nc.vector.tensor_reduce(st[:, 24:34], heads(nrm), AX, ALU.add).then_inc(S("qk_ss", g), 1)
                    dve.wait_ge(S("qk_rms", g), b + 1)
                    chain(nc.vector.reciprocal(st[:, 24:34], st[:, 34:44]))
                    chain(nc.vector.tensor_tensor(heads(nrm), heads(raw[:, 0:QK]), st[:, 24:34].unsqueeze(2).to_broadcast([P, 10, HD]), ALU.mult))
                    if b:
                        box, use = boxes[("qkT", g, b - 1)]
                        dve.wait_ge(box_ready[box], use + 1)
                    if g == CTX:
                        chain(nc.vector.tensor_tensor(rot, nrm, gain, ALU.mult))
                    else:
                        chain(nc.vector.tensor_tensor(nrm, nrm, gain, ALU.mult))
                        pair = nrm.rearrange("p (h d e) -> p h d e", h=10, e=2)
                        out = rot.rearrange("p (h d e) -> p h d e", h=10, e=2)
                        cos = rope[:, b, 0, :].unsqueeze(1).to_broadcast([P, 10, 32])
                        sin = rope[:, b, 1, :].unsqueeze(1).to_broadcast([P, 10, 32])
                        for e, (m1, m2, op) in enumerate(((cos, sin, ALU.subtract), (sin, cos, ALU.add))):
                            nc.vector.tensor_tensor(heads(rt1), pair[:, :, :, 0], m1, ALU.mult)
                            chain(nc.vector.tensor_tensor(heads(rt2), pair[:, :, :, 1], m2, ALU.mult))
                            chain(nc.vector.tensor_tensor(out[:, :, :, e], heads(rt1), heads(rt2), op))
                    dup(rot[:, 512:640], g).then_inc(S("rot", g), 1)

            def conv(g, lo, hi):
                t = tokens(g)
                u, out = conv_u(g), conv_out(g)
                if lo == 0:
                    given(dve, ("vg", g, 3))
                    given(dve, ("cwT", 0, g))
                    box, use = boxes[("qkv", g, len(BLOCKS[g]) - 1)]
                    dve.wait_ge(box_ready[box], use + 1)
                for j in range(lo, hi):
                    for c in range(4):
                        if j == 0:
                            ins = nc.vector.tensor_scalar(out[:, c, :], u[:, c, 0:t], cw[:, c, 0:1], cw[:, c, CONVK:CONVK + 1],
                                                          ALU.mult, ALU.add)
                        else:
                            dve.wait_ge(S("conv", g), 4 * j + c - 3)
                            ins = nc.vector.scalar_tensor_tensor(out[:, c, :], u[:, c, j:j + t], cw[:, c, j:j + 1], out[:, c, :],
                                                                 ALU.mult, ALU.add)
                        ins.then_inc(S("conv", g), 1)

            def attend(g, b, taps):
                nk = n_keys(g)
                for h in range(HEADS):
                    n = b * HEADS + h
                    box = take(dve, ("S", g, b, h))
                    chain(nc.vector.tensor_reduce(st[:, 44 + n % 2:45 + n % 2], box[:, 0:nk], AX, ALU.max))
                    nc.vector.tensor_scalar(st[:, 46 + n % 2:47 + n % 2], st[:, 44 + n % 2:45 + n % 2], -HD ** -0.5, None,
                                            ALU.mult).then_inc(S("row_max", g), 1)
                    lo = taps[0] + (taps[1] - taps[0]) * h // HEADS
                    hi = taps[0] + (taps[1] - taps[0]) * (h + 1) // HEADS
                    conv(g, lo, hi)
                    given(dve, ("S", g, b, h))
                    chain(nc.vector.reciprocal(st[:, 50 + n % 2:51 + n % 2], st[:, 48 + n % 2:49 + n % 2]))
                    box = take(dve, ("O", g, b, h))
                    if h == 0 and b:
                        bx, use = boxes[("oT", g, b - 1)]
                        dve.wait_ge(box_ready[bx], use + 1)
                    give(nc.vector.tensor_scalar(o_tok[:, h * HD:(h + 1) * HD], box[:, 0:HD], st[:, 50 + n % 2:51 + n % 2], None,
                                                 ALU.mult), ("O", g, b, h))

            def conv_norm(g):
                t = tokens(g)
                out = conv_out(g)
                box = take(dve, ("mean", g))
                dve.wait_ge(S("conv", g), 4 * CONVK)
                give(nc.vector.tensor_tensor(out, out, box[:, 0:t].unsqueeze(1).to_broadcast([P, 4, t]), ALU.subtract), ("mean", g))
                given(dve, ("var", g))
                chain(nc.vector.reciprocal(small(0)[:, 0:t], small(1)[:, 0:t]))
                nc.vector.tensor_tensor(out, out, small(0)[:, 0:t].unsqueeze(1).to_broadcast([P, 4, t]), ALU.mult).then_inc(S("conv_unit", g), 1)

            def odd_a(g):
                t = tokens(g)
                given(dve, ("cwT", 1, g))
                nc.vector.memset(s_pad[:, 0:1], 0.0)
                chain(nc.vector.memset(s_pad[:, t + 1:t + 2], 0.0))
                for c in range(4):
                    dve.wait_ge(S("gc", g), c + 1)
                    box = take(dve, ("cv", g, c))
                    give(nc.vector.tensor_tensor(s_pad[:, 1:t + 1], gc_sb[:, 0:t], box[:, 512:512 + t], ALU.mult), ("cv", g, c))
                    given(dve, ("cv", g, c))
                    dst = cat(g)[:, 4 + c, :]
                    chain(nc.vector.tensor_scalar(dst, s_pad[:, 0:t], cw_odd[:, c, 0:1], None, ALU.mult))
                    for j in (1, 2):
                        chain(nc.vector.scalar_tensor_tensor(dst, s_pad[:, j:j + t], cw_odd[:, c, j:j + 1], dst, ALU.mult, ALU.add))
                    box = take(dve, ("gb", g, c))
                    give(nc.vector.tensor_tensor(dst, dst, box[:, 0:t], ALU.mult), ("gb", g, c))

            def mix_out(l, g):
                nb = len(BLOCKS[g])
                dve.wait_ge(S("bc_gate", l, g), 16)
                n = 0
                for s in range(4):
                    for b in range(nb):
                        box = take(dve, ("out", l, g, s, b))
                        tmp = small(n)[:, 0:WC]
                        give(nc.vector.tensor_tensor(tmp, box[:, 0:WC], BC[:, 0, s * WC:(s + 1) * WC], ALU.mult), ("out", l, g, s, b))
                        given(dve, ("out", l, g, s, b))
                        x = XM[:, b, s * WC:(s + 1) * WC]
                        last = nc.vector.tensor_tensor(x, x, tmp, ALU.add)
                        n += 1
                        if n < 4 * nb:
                            chain(last)
                last.then_inc(S("x_mixed", l, g), 1)

            mod(0)
            norm(0, CTX, "hT")
            even_a(CTX)
            even_qkv(CTX)
            attend(CTX, 0, (0, CONVK))
            conv_norm(CTX)
            mix_out(0, CTX)
            norm(0, CTX, "h2T")
            topk(0, 0, 0)
            topk(0, 1, 0)
            step(0, 0, 0)
            norm(0, SMP, "hT")
            step(0, 1, 0)
            even_a(SMP)
            step(0, 2, 0)
            even_qkv(SMP)
            for b in range(3):
                step(0, 3 + b, 0)
                attend(SMP, b, (8 * b, 8 * b + 8))
            step(0, 6, 0, nxt=False)
            attend(SMP, 3, (24, CONVK))
            conv_norm(SMP)
            step(0, 7, 0, nxt=False)
            mix_out(0, SMP)
            norm(0, SMP, "h2T")
            topk(1, 0, 0)
            topk(1, 1, 0)
            step(1, 0, 0, ends=0)
            step(1, 1, 0)
            mod(1)
            step(1, 2, 0)
            norm(1, CTX, "hT")
            odd_a(CTX)
            step(1, 3, 0)
            step(1, 4, 0)
            mix_out(1, CTX)
            step(1, 5, 0, nxt=False)
            norm(1, CTX, "h2T")
            topk(1, 7, 0)
            step(1, 6, 0)
            step(1, 7, 0)
            with Segments(dve, 2, 4, per_seg) as seg:
                chain.restart()
                for h in range(HEADS):
                    step(seg, h, 0, ends=seg - 1 if h == 0 else None)
            for h in range(HEADS):
                step(4, h, 0 if h < 6 else 1, ends=3 if h == 0 else None)
            step(5, 0, 1, ends=4)
            step(5, 1, 1)
            norm(1, SMP, "hT")
            step(5, 2, 1)
            odd_a(SMP)
            step(5, 3, 1)
            step(5, 4, 1)
            mix_out(1, SMP)
            step(5, 5, 1)
            norm(1, SMP, "h2T")
            step(5, 6, 1, nxt=False)
            step(5, 7, 1, nxt=False)
            topk(6, 0, 1)
            topk(6, 1, 1)
            with Segments(dve, 6, 9, per_seg) as seg:
                chain.restart()
                for h in range(HEADS):
                    step(seg, h, 1, ends=seg - 1 if h == 0 else None, l_ends=1)
            for h in range(HEADS):
                step(9, h, 1, ends=8 if h == 0 else None, l_ends=1, nxt=h < 6)
            seg_end(9, 1)


_INS = ["x_prompt", "x_sample", "cache_k", "cache_v", "c", "c_ctx", "w_mod", "b_mod", "norm_mix_g", "norm_ffn_g",
        "w_in_even", "w_out_even", "conv_dw_w", "conv_dw_b", "conv_ln_g", "conv_ln_b", "q_norm_g", "k_norm_g",
        "w_in_odd", "w_out_odd", "short_conv_w", "peer_wq", "peer_keys", "peer_u", "peer_v", "final_norm_g"]
_OUTS = [(1, P, D), (1, 4 * P, D), (1, 1, P, 2, HD), (1, 1, P, 2, HD)]


def shape_tables():
    def dft(n):
        a = 2 * np.pi * (np.outer(np.arange(n), np.arange(n)) % n) / n
        return np.cos(a) / np.sqrt(n), np.sin(a) / np.sqrt(n)

    c, s = dft(P)
    out = {"ident": np.eye(P), "dft_ch": np.concatenate([c, s], 1), "iota16": np.tile(np.arange(16.0), (P, 1))}
    for name, n in (("dft_ctx", P), ("dft_smp", 4 * P)):
        c, s = dft(n)
        out[name] = np.stack([c, -s]).reshape(2, n // P, P, n).transpose(2, 0, 1, 3)
    grid_w, half, theta = 64, HD // 2, 10000.0
    inv = np.float32(theta) ** (-np.arange(0, half, 2, dtype=np.float32) / half)
    t = np.arange(4 * P)
    ang = np.concatenate([(t // grid_w).astype(np.float32)[:, None] * inv, (t % grid_w).astype(np.float32)[:, None] * inv], 1)
    r = np.stack([np.cos(ang), np.sin(ang)], 1)
    out["rope"] = r.reshape(4, P, 2, half).transpose(1, 0, 2, 3)
    mask = np.zeros((2, 6, 8))
    mask[:, [1, 4]] = 1.0
    out["scale_rows"] = mask.reshape(96, 1)
    return {k: np.ascontiguousarray(v.astype(np.float32)) for k, v in out.items()}


def kernel(**inputs):
    import numpy as _np
    import concourse.bacc as _bacc
    from concourse import mybir as _mybir
    from concourse.bass_utils import run_bass_kernel_spmd as _run

    nc = _bacc.Bacc("TRN2", target_bir_lowering=False, num_devices=1)
    arrays, args = {}, {}
    given = {name: _np.ascontiguousarray(inputs[name]) for name in _INS}
    for name, a in list(given.items()) + list(shape_tables().items()):
        arrays[f"in_{name}_dram"] = a
        args[name] = nc.dram_tensor(f"in_{name}_dram", a.shape, _mybir.dt.from_np(a.dtype), kind="ExternalInput").ap()
    outs = [nc.dram_tensor(f"out_{i}_dram", shape, _mybir.dt.float32, kind="ExternalOutput").ap()
            for i, shape in enumerate(_OUTS)]
    build(nc, args, outs)
    r = _run(nc, [arrays], core_ids=[0])
    return tuple(r.results[0][f"out_{i}_dram"] for i in range(len(_OUTS)))
```

```python
from contextlib import ExitStack

import numpy as np
import concourse.bass as bass
from concourse import mybir

F32 = mybir.dt.float32
U32 = mybir.dt.uint32
ALU = mybir.AluOpType
ACT = mybir.ActivationFunctionType
AX = mybir.AxisListType.X

P = 128
D = 1024
DC = D // P
HEADS = 8
TOPK = 16
KEYS = 128
EXPERTS = KEYS * KEYS
EPS = 1e-6
NU = 8
NV = 8
NW = 3
WC = 256
NDIAG = 4
NEG = -3.0e38
CONVK = 31
CW_ROWS = CONVK + 3
PAD = CONVK // 2
HD = 64
QK = 640
BOX = 1024
CTX, SMP = 0, 1
BLOCKS = {CTX: [0], SMP: [1, 2, 3, 4]}
MOD_SLICES = ((0, 8), (8, 24))
RATES = {(0, SMP): {"norm": 1, "vg": 2, "vg_end": 8, "qkv": 4, "attend": 1, "conv_norm": 4, "out": 1, "out_end": 6, "slice": 4,
                    "enter": 4},
         (1, CTX): {"norm": 2, "f": 1, "cv": 2, "Y": 1, "ff": 1, "out": 1, "slice": 4},
         (1, SMP): {"start": 8, "norm": 1, "f": 2, "f_end": 4, "cv": 4, "cv_end": 8, "Y": 1, "ff": 2, "out": 1, "out_end": 6,
                    "slice": 4, "enter": 4}}
MOD_RATE = 2
ROWS = HEADS * TOPK
VECTOR_RANKS = (1, 2, 4, 5, 6, 8, 9, 10, 12, 13, 14)
VECTOR_ROWS = [(seg, r) for seg, n in ((0, ROWS), (1, ROWS - 2 * TOPK), (5, ROWS), (6, ROWS - 2 * TOPK))
               for r in range(n) if r % TOPK in VECTOR_RANKS and not (seg == 0 and 36 <= r < 68)]


def behind(seg, r):
    if r >= TOPK:
        return seg, r - TOPK
    if isinstance(seg, int) and seg == 0:
        return None
    return seg - 1, r + ROWS - TOPK


def by_vector(seg, r):
    return isinstance(seg, int) and (seg, r) in VECTOR_ROWS


def vector_count(n):
    return sum(seg * ROWS + r < n for seg, r in VECTOR_ROWS)


def plan_boxes():
    keys = []

    def mod(l, part):
        if part == 0:
            keys.append(("condT", l))
        if l:
            keys.append(("mod", l, part))
        keys.append(("modT", l, part))

    def mix(l, g):
        nb = len(BLOCKS[g])
        keys.append(("cwT", l, g))
        for b in range(nb):
            keys.append(("hT", l, g, b))
        if l == 0:
            for c in range(4):
                keys.append(("vg", g, c))
            if g == SMP:
                keys.append(("ckT", g))
            keys.append(("qkv", g, 0))
            for b in range(nb):
                if b + 1 < nb:
                    keys.append(("qkv", g, b + 1))
                keys.append(("qkT", g, b))
            for b in range(nb):
                keys.append(("S", g, b, 0))
                for h in range(HEADS):
                    if h < HEADS - 1:
                        keys.append(("S", g, b, h + 1))
                    keys.append(("PT", g, b, h))
                    keys.append(("O", g, b, h))
                keys.append(("oT", g, b))
            if g == CTX:
                mod(0, 1)
            keys.append(("mean", g))
            keys.append(("var", g))
        else:
            for c in range(4):
                keys.append(("fT", g, c))
            for c in range(4):
                keys.append(("cv", g, c))
                keys.append(("gb", g, c))
            for b in range(nb):
                keys.append(("Y", g, b))
            for c in range(4):
                keys.append(("ffT", g, c))
        for s in range(4):
            for b in range(nb):
                keys.append(("out", l, g, s, b))
        for b in range(nb):
            keys.append(("h2T", l, g, b))
        for s in range(8):
            keys.append(("kyT", l, g, s))
            for name in ("q", "sc"):
                for j in range(2):
                    keys.append((name, l, g, 2 * s + j))

    mod(0, 0)
    mix(0, CTX)
    mix(0, SMP)
    mod(1, 0)
    mod(1, 1)
    mix(1, CTX)
    mix(1, SMP)
    return {k: (n % 3, n // 3) for n, k in enumerate(keys)}


def plan_weights():
    order = []

    def mod(l, part):
        for s in range(*MOD_SLICES[part]):
            order.append((("wmod", l, s), ("modT", l, part), 1))

    def mix(l, g):
        nb = len(BLOCKS[g])
        if l == 0:
            for s, c in ((0, 1), (2, 1), (1, 3), (3, 3)):
                order.append((("win", l, g, s), ("vg", g, c), 1))
            for s in (4, 5, 6):
                order.append((("win", l, g, s), ("qkv", g, nb - 1), 1))
            if g == CTX:
                mod(0, 1)
        else:
            for s in (0, 1):
                order.append((("win", l, g, s), ("fT", g, 2 * s + 1), 1))
            for half in (0, 1):
                for s in (2, 4, 6):
                    order.append((("win", l, g, s + half), ("gb", g, 2 * half + 1), 1))
        for s in range(4):
            order.append((("wout", l, g, s), ("out", l, g, s, nb - 1), 1))
        for s in range(8):
            order.append((("wq", l, g, s), ("q", l, g, 2 * s + 1), 2))

    mod(0, 0)
    mix(0, CTX)
    mix(0, SMP)
    mod(1, 0)
    mod(1, 1)
    mix(1, CTX)
    mix(1, SMP)
    plan, counts = {}, [0] * NW
    for n, (key, last, dmas) in enumerate(order):
        slot = n % NW
        counts[slot] += 16 * dmas
        before = order[n - NW] if n >= NW else None
        plan[key] = (slot, counts[slot], before)
    return plan


def build(nc, T, outs):
    boxes = plan_boxes()
    weights = plan_weights()
    y_prompt, y_sample, new_k, new_v = outs

    with ExitStack() as ctx:
        def sb(name, shape, dt=F32):
            return ctx.enter_context(nc.sbuf_tensor(name, shape, dt))

        def sem(name):
            return ctx.enter_context(nc.semaphore(name))

        def dram(name, shape):
            return nc.dram_tensor(name, shape, F32, kind="Internal").ap()

        modrow = dram("modrow", [2, 2, 6, D])
        xa = dram("xa", [10, P, D])
        xb = dram("xb", [5, P, D])
        hs = dram("hs", [10, P, D])
        sc = dram("sc", [80, P, 2, KEYS])

        ident = sb("ident", [P, P])
        ones = sb("ones", [P, P])
        dft_ch = sb("dft_ch", [P, 2 * P])
        rope = sb("rope", [P, 4, 2, 32])
        iota16 = sb("iota16", [P, 16])
        eps = sb("eps", [P, 1])
        u_ring = sb("u_ring", [P, NU, D])
        v_ring = sb("v_ring", [P, NV, D])
        w_slots = sb("w_slots", [P, NW, DC * WC + 2 * P])
        h_cur = sb("h_cur", [P, D])
        h_next = sb("h_next", [P, D])
        x_seg = sb("x_seg", [P, D])
        g_seg = sb("g_seg", [P, D])
        t_seg = sb("t_seg", [P, D])
        s_buf = sb("s_buf", [P, 2, 2, KEYS])
        diag = sb("diag", [P, NDIAG, P])
        sv = sb("sv", [P, 2, TOPK])
        si = sb("si", [P, 2, TOPK], U32)
        sif = sb("sif", [P, 2, TOPK])
        cand = sb("cand", [P, 16, 16])
        fv = sb("fv", [P, 2, TOPK])
        fi = sb("fi", [P, TOPK], U32)
        ab = sb("ab", [P, 2, TOPK], U32)
        abf = sb("abf", [P, 2, TOPK])
        onehot = sb("onehot", [P, 2, 16, 16])
        cand_rep = onehot[:, 0].rearrange("p a b -> p (a b)")
        s_rep = onehot[:, 1].rearrange("p a (h b) -> p (a h b)", h=1).rearrange("p (j k) -> p j k", j=2)
        e01 = sb("e01", [P, 2, TOPK])
        neg_max = sb("neg_max", [P, 2])
        idx = sb("idx", [P, 4, TOPK], U32)
        ex = sb("ex", [P, 4, TOPK])
        ex_sum = sb("ex_sum", [P, 4])
        ex_rec = sb("ex_rec", [P, 4])
        act_v = sb("act_v", [P, 2, TOPK])
        gelu_v = sb("gelu_v", [P, 2, TOPK])
        w_v = sb("w_v", [P, 2, TOPK])
        seg_st = sb("seg_st", [P, 4])
        XM = sb("XM", [P, 4, D])
        HT = sb("HT", [P, 4096])
        CAT = sb("CAT", [P, 4096])
        BC = sb("BC", [P, 2, D])
        AR = sb("AR", [P, 7300])
        st = sb("st", [P, 64])

        ps_v = ctx.enter_context(nc.psum_tensor("ps_v", [P, D], F32))
        ps_box = [ctx.enter_context(nc.psum_tensor(f"ps_box{i}", [P, BOX], F32)) for i in range(3)]

        const_in = sem("const_in")
        u_landed = [sem(f"u_landed{i}") for i in range(NU)]
        v_landed = [sem(f"v_landed{i}") for i in range(NV)]
        dots_done = sem("dots_done")
        vsum_done = sem("vsum_done")
        vector_sum = sem("vector_sum")
        acc_free = sem("acc_free")
        s_landed = [sem("s_landed0"), sem("s_landed1")]
        topk_done = sem("topk_done")
        negmax_done = sem("negmax_done")
        exp_done = sem("exp_done")
        gelu_done = sem("gelu_done")
        w_done = sem("w_done")
        diag_done = sem("diag_done")
        h_landed = sem("h_landed")
        h_ready = sem("h_ready")
        seg_landed = sem("seg_landed")
        x_new = sem("x_new")
        ss_done = sem("ss_done")
        y_new = sem("y_new")
        x_stored = sem("x_stored")
        fg_landed = sem("fg_landed")
        dve_chain = sem("dve_chain")
        act_chain = sem("act_chain")
        box_ready = [sem(f"box_ready{i}") for i in range(3)]
        box_free = [sem(f"box_free{i}") for i in range(3)]
        w_landed = [sem(f"w_landed{i}") for i in range(NW)]

        named = {}

        def S(*key):
            name = "_".join(str(k) for k in key)
            if name not in named:
                named[name] = sem(name)
            return named[name]

        def wait(eng, s, n, use=""):
            if isinstance(n, int):
                if s in (vsum_done, diag_done) and n > 0:
                    n -= vector_count(n)
                if n > 0:
                    eng.wait_ge(s, n)
            else:
                n.loop.wait(s, n, use)

        class Count:
            def __init__(self, loop, per_seg, base):
                self.loop, self.per_seg, self.base = loop, per_seg, base

            def __add__(self, n):
                return Count(self.loop, self.per_seg, self.base + n)

            def __sub__(self, n):
                return self + -n

            def __mul__(self, n):
                return Count(self.loop, self.per_seg * n, self.base * n)

            __radd__, __rmul__ = __add__, __mul__

            def value(self):
                return self.loop.seg * self.per_seg + self.base

        class Segments:
            def __init__(self, eng, lo, hi, counts):
                self.eng, self.lo, self.hi, self.counts = eng, lo, hi, counts

            def __enter__(self):
                self.at = {}
                for key, (per_seg, first) in self.counts.items():
                    if per_seg * self.lo + first > 0:
                        skipped = vector_count(self.lo * ROWS) if key[0] in (vsum_done, diag_done) else 0
                        reg = self.eng.alloc_register(f"{key[0].name}_{key[1]}_{self.lo}_wanted")
                        self.eng.reg_mov(reg, per_seg * self.lo + first - skipped)
                        self.at[key] = [reg, first]
                self.fori = self.eng.Fori(self.lo, self.hi)
                self.seg = self.fori.__enter__()
                return Count(self, 1, 0)

            def wait(self, s, n, use):
                per_seg, _ = self.counts[s, use]
                reg, at = self.at[s, use]
                assert n.per_seg == per_seg and n.base >= at
                if n.base != at:
                    self.eng.reg_add(reg, reg, n.base - at)
                self.eng.wait_ge(s, reg)
                self.eng.reg_add(reg, reg, 1)
                self.at[s, use][1] = n.base + 1

            def __exit__(self, *exc):
                for key, (reg, at) in self.at.items():
                    per_seg, first = self.counts[key]
                    if at not in (first, first + per_seg):
                        self.eng.reg_add(reg, reg, per_seg + first - at)
                return self.fori.__exit__(*exc)

        class Chain:
            def __init__(self, eng, s):
                self.eng, self.s, self.n = eng, s, 0

            def __call__(self, ins):
                self.n += 1
                ins.then_inc(self.s, 1)
                self.eng.wait_ge(self.s, self.n)

            def restart(self):
                self.eng.sem_clear(self.s)
                self.n = 0

        def rate(l, g, name):
            return RATES.get((l, g), {}).get(name, 0)

        def stored(eng, l, g, h):
            eng.wait_ge(S("stage_out", l, g, h % 2), 16 * len(BLOCKS[g]) * (h // 2 + 1))

        def index(n):
            return n if isinstance(n, int) else n.value()

        def fill(pe, key):
            box, use = boxes[key]
            if use:
                pe.wait_ge(box_free[box], use)
            return ps_box[box]

        def filled(ins, key):
            ins.then_inc(box_ready[boxes[key][0]], 1)

        def take(eng, key):
            box, use = boxes[key]
            eng.wait_ge(box_ready[box], use + 1)
            return ps_box[box]

        def give(ins, key):
            ins.then_inc(box_free[boxes[key][0]], 1)

        def given(eng, key):
            box, use = boxes[key]
            eng.wait_ge(box_free[box], use + 1)

        def weight(pe, key):
            slot, count, _ = weights[key]
            pe.wait_ge(w_landed[slot], count)
            return w_slots[:, slot, 0:DC * WC].rearrange("p (c n) -> p c n", c=DC)

        def weight_keys(key):
            return w_slots[:, weights[key][0], DC * WC:DC * WC + 2 * P].rearrange("p (j d) -> p j d", j=2)

        def load_weight(sp, key, src, col, extra=None):
            slot, _, before = weights[key]
            if key[0] == "wmod" and before is not None and before[0][0] == "wmod":
                sp.wait_ge(S("wmod_read", key[1]), before[0][2] + 1)
            elif before is not None:
                box, use = boxes[before[1]]
                sp.wait_ge(box_ready[box], use + 1)
            view = w_slots[:, slot, 0:DC * WC].rearrange("p (c n) -> p c n", c=DC)
            sp.dma_start(view, src.rearrange("(c p) n -> p c n", p=P)[:, :, col:col + WC]).then_inc(w_landed[slot], 16)
            if extra is not None:
                sp.dma_start(weight_keys(key), extra).then_inc(w_landed[slot], 16)

        def tokens(g):
            return P * len(BLOCKS[g])

        def ht(g):
            return HT[:, 0:8 * tokens(g)].rearrange("p (c t) -> p c t", c=8)

        def cat(g):
            return CAT[:, 0:8 * tokens(g)].rearrange("p (c t) -> p c t", c=8)

        def seg_of(l, g, b):
            return 5 * l + BLOCKS[g][b]

        def conv_u(g):
            t = tokens(g)
            return AR[:, 0:4 * (t + 2 * PAD)].rearrange("p (c t) -> p c t", c=4)

        Q_AT, K_AT, V_AT, MU_AT, RS_AT, CW_AT = 2168, 4216, 5496, 6136, 6648, 7160

        def q_t(g):
            return AR[:, Q_AT:Q_AT + 4 * tokens(g)].rearrange("p (c t) -> p c t", c=4)

        def n_keys(g):
            return tokens(g) + (P if g == SMP else 0)

        def k_t(g):
            return AR[:, K_AT:K_AT + 2 * n_keys(g)].rearrange("p (v t) -> p v t", v=2)

        v_t = AR[:, V_AT:V_AT + 640].rearrange("p (b n) -> p b n", b=5)
        cw = AR[:, CW_AT:CW_AT + 4 * CW_ROWS].rearrange("p (c r) -> p c r", c=4)
        raw = CAT[:, 0:768]
        nrm = CAT[:, 768:768 + QK]
        rot = CAT[:, 1408:1408 + QK]
        kdup = CAT[:, 2048:2304]
        gain = CAT[:, 2304:2304 + QK]
        rt1 = CAT[:, 2944:3264]
        rt2 = CAT[:, 3264:3584]
        cw_raw = CAT[0:CW_ROWS, 3584:4096]
        prob = HT[:, 2048:2688]
        prob_t = HT[:, 2688:3328].rearrange("p (b n) -> p b n", b=5)
        o_tok = HT[:, 3328:3840]

        def h_tile(b):
            return CAT[:, (b % 2) * D:(b % 2) * D + D]

        def small(b):
            return AR[:, MU_AT + 512 * (b % 2):MU_AT + 512 * (b % 2) + 512]

        def conv_out(g):
            return HT[:, 0:4 * tokens(g)].rearrange("p (c t) -> p c t", c=4)

        def conv_sq(g):
            return AR[:, 0:4 * tokens(g)].rearrange("p (c t) -> p c t", c=4)

        def f_t(g):
            return AR[:, 0:4 * tokens(g)].rearrange("p (c t) -> p c t", c=4)

        def y_tok(g):
            n = len(BLOCKS[g])
            return AR[:, 2048:2048 + n * 1024].rearrange("p (b g n) -> p b g n", b=n, g=4)

        gc_sb = AR[:, 6144:6656]
        s_pad = AR[:, 6656:7170]
        cw_odd = AR[:, 7170:7182].rearrange("p (c r) -> p c r", c=4)
        def dft_t(g):
            n = len(BLOCKS[g])
            return HT[:, 0:2 * n * tokens(g)].rearrange("p (s b t) -> p s b t", s=2, b=n)

        def q_sb(g, j):
            return AR[:, j * 512:j * 512 + tokens(g)]

        ky_sb = AR[:, 1024:1280].rearrange("p (j k) -> p j k", j=2)

        def stage(g, j):
            n = len(BLOCKS[g])
            return AR[:, 1280 + 1024 * j:1280 + 1024 * j + n * 256].rearrange("p (b j k) -> p b j k", b=n, j=2)

        def v_acc(seg):
            return t_seg[:, :] if seg in (0, 5) else CAT[:, 0:D]

        cond_raw = AR[0:16, 0:P]

        def cond_t(l):
            return u_ring[:, 1, 0:16] if l == 0 else AR[:, 128:144]

        def mod_at(l, part, what):
            base = u_ring[:, 2 * part, :] if l == 0 else AR[:, 256 + 640 * part:896 + 640 * part]
            rows = 2 * 2 * (MOD_SLICES[part][1] - MOD_SLICES[part][0])
            at = {"sb": 0, "row": 128, "bias": 256, "gain": 384, "mask": 512}[what]
            if what == "sb":
                return base[:, at:at + rows]
            return base[0:rows, at:at + (1 if what == "mask" else P)]

        block = ctx.enter_context(nc.Block())

        @block.sync
        def _(sp):
            per_seg = {(h_ready, ""): (1, 1), (x_new, ""): (1, 0), (y_new, ""): (1, -5), (x_stored, ""): (16, 0)}
            for dst, src in ((ident, "ident"), (dft_ch, "dft_ch"), (iota16, "iota16"), (rope, "rope")):
                sp.dma_start(dst[:], T[src]).then_inc(const_in, 16)

            def mod_in(l):
                sp.dma_start(cond_raw[0:8, :], T["c_ctx"].rearrange("(k p) -> k p", p=P)).then_inc(S("cond_in", l), 16)
                sp.dma_start(cond_raw[8:16, :], T["c"][0].rearrange("(k p) -> k p", p=P)).then_inc(S("cond_in", l), 16)

            def mod_rows_in(l):
                sp.wait_ge(S("gain_one", l), 2)
                for part, (lo, hi) in enumerate(MOD_SLICES):
                    n = 2 * (hi - lo)
                    for g in range(2):
                        sp.dma_start(mod_at(l, part, "bias")[n * g:n * g + n, :],
                                     T["b_mod"][l].rearrange("(k p) -> k p", p=P)[2 * lo:2 * hi]).then_inc(S("mod_in", l), 16)
                        row = n * g + (8 if part == 0 else 16)
                        sp.dma_start(mod_at(l, part, "gain")[row:row + 8, :],
                                     T["norm_ffn_g" if part else "norm_mix_g"][l].rearrange("(k p) -> k p", p=P)).then_inc(S("mod_in", l), 16)
                    sp.dma_start(mod_at(l, part, "mask"), T[f"scale_rows{part}"]).then_inc(S("mod_in", l), 16)

            def mod(l, part):
                for s in range(*MOD_SLICES[part]):
                    load_weight(sp, ("wmod", l, s), T["w_mod"][l], s * WC)

            def mod_out(l, part):
                lo, hi = (m // 4 for m in MOD_SLICES[part])
                n = 8 * (hi - lo)
                sp.wait_ge(S("mod_row", l), part + 1)
                for g in range(2):
                    sp.dma_start(modrow[l, g, lo:hi].rearrange("m (k p) -> (m k) p", p=P),
                                 mod_at(l, part, "row")[n * g:n * g + n, :]).then_inc(S("mod_out", l), 16)
                sp.wait_ge(S("mod_out", l), 32 * (part + 1))

            def load_bc(l, g, m, slot, name):
                sp.dma_start(BC[:, slot, :], modrow[l, g, m].partition_broadcast(P)).then_inc(S(name, l, g), 16)

            def mix_in(l, g):
                x_in(l, g)
                bc_in(l, g)

            def bc_in(l, g):
                load_bc(l, g, 1, 0, "bc_in")
                load_bc(l, g, 0, 1, "bc_in")

            def x_in(l, g):
                for b in range(len(BLOCKS[g])):
                    if l == 1:
                        src = xb[BLOCKS[g][b]]
                    else:
                        src = T["x_prompt" if g == CTX else "x_sample"][0, b * P:(b + 1) * P, :]
                    sp.dma_start(XM[:, b, :], src).then_inc(S("xm_in", l, g), 16)
                if l == 0:
                    sp.dma_start(cw_raw[0:CONVK, :], T["conv_dw_w"][0]).then_inc(S("cw_in", l, g), 16)
                    for j, name in enumerate(("conv_dw_b", "conv_ln_g", "conv_ln_b")):
                        sp.dma_start(cw_raw[CONVK + j:CONVK + j + 1, :], T[name]).then_inc(S("cw_in", l, g), 16)
                    for h in range(10):
                        sp.dma_start(gain[:, HD * h:HD * (h + 1)],
                                     T["q_norm_g" if h < 8 else "k_norm_g"][0].partition_broadcast(P)).then_inc(S("gain_in", g), 16)
                else:
                    sp.dma_start(cw_raw[0:3, :], T["short_conv_w"][0]).then_inc(S("cw_in", l, g), 16)

            def even_in(g):
                w = T["w_in_even"][0]
                for s in (0, 2, 1, 3, 4, 5, 6):
                    load_weight(sp, ("win", 0, g, s), w, s * WC)
                    if s == 3 and g == SMP:
                        box, use = boxes[("hT", 0, g, 3)]
                        sp.wait_ge(box_ready[box], use + 1)
                        sp.dma_start(raw[:, 512:640], T["cache_k"][0, 0].rearrange("t v d -> t (v d)")).then_inc(S("cache_in"), 16)
                        sp.dma_start(v_t[:, 0, :], T["cache_v"][0, 0].rearrange("t v d -> t (v d)")).then_inc(S("cache_in"), 16)

            def kv_out():
                sp.wait_ge(S("rot", CTX), 1)
                sp.dma_start(new_k[0, 0].rearrange("t v d -> t (v d)"), rot[:, 512:640]).then_inc(S("kv_out"), 16)
                sp.dma_start(new_v[0, 0].rearrange("t v d -> t (v d)"), v_t[:, 0, :]).then_inc(S("kv_out"), 16)
                sp.wait_ge(S("kv_out"), 32)

            def odd_in(g):
                for s in (0, 1, 2, 4, 6, 3, 5, 7):
                    load_weight(sp, ("win", 1, g, s), T["w_in_odd"][0], s * WC)
                box, use = boxes[("gb", g, 3)]
                sp.wait_ge(box_ready[box], use + 1)
                sp.dma_start(dft_t(g), T["dft_ctx" if g == CTX else "dft_smp"]).then_inc(S("dft_in", g), 16)

            def out_in(l, g):
                nb = len(BLOCKS[g])
                sp.wait_ge(S("h_tok", l, g), nb)
                load_bc(l, g, 2, 0, "bc_gate")
                for s in range(4):
                    load_weight(sp, ("wout", l, g, s), T["w_out_even" if l == 0 else "w_out_odd"][0], s * WC)
                sp.wait_ge(S("x_mixed", l, g), 1)
                load_bc(l, g, 4, 0, "bc_ffn")
                load_bc(l, g, 3, 1, "bc_ffn")
                for b in range(nb):
                    sp.dma_start(xa[seg_of(l, g, b)], XM[:, b, :]).then_inc(S("xa_out", l, g), 16)

            def prep(l, g):
                nb = len(BLOCKS[g])
                for s in range(8):
                    load_weight(sp, ("wq", l, g, s), T["peer_wq"][l], s * WC,
                                extra=T["peer_keys"][l].rearrange("h j k d -> k (h j) d")[:, 2 * s:2 * s + 2, :])
                    if s == 1:
                        for b in range(nb):
                            sp.wait_ge(S("h2_tok", l, g), b + 1)
                            sp.dma_start(hs[seg_of(l, g, b)], XM[:, b, :]).then_inc(S("hs_out", l, g), 16)
                        sp.wait_ge(S("hs_out", l, g), 16 * nb)
                        sp.wait_ge(S("xa_out", l, g), 16 * nb)
                        if (l, g) == (0, CTX):
                            load_h(0)
                            load_seg(0, 0, CTX)
                        elif g == SMP:
                            load_h(5 * l + 1)
                        if (l, g) == (1, SMP):
                            sp.dma_start(BC[:, 0, :], T["final_norm_g"].partition_broadcast(P)).then_inc(fg_landed, 16)

            def prep_end(l, g):
                for h in (6, 7):
                    stored(sp, l, g, h)

            def load_h(seg):
                wait(sp, h_ready, seg)
                sp.dma_start(h_next[:, :], hs[index(seg)]).then_inc(h_landed, 16)

            def load_seg(seg, l, g):
                sp.dma_start(x_seg[:, :], xa[index(seg)]).then_inc(seg_landed, 16)
                sp.dma_start(g_seg[:, :], modrow[l, g, 5].partition_broadcast(P)).then_inc(seg_landed, 16)

            def store_seg(seg, l):
                if l == 0:
                    wait(sp, x_new, seg + 1)
                    sp.dma_start(xb[index(seg)], x_seg[:, :]).then_inc(x_stored, 16)
                else:
                    wait(sp, y_new, seg - 4)
                    dst = y_prompt[0] if isinstance(seg, int) and seg == 5 else y_sample[0].rearrange("(b p) d -> b p d", p=P)[index(seg - 6)]
                    sp.dma_start(dst, t_seg[:, :]).then_inc(x_stored, 16)
                wait(sp, x_stored, 16 * (seg + 1))

            def segment(seg, l, g, l_before):
                load_h(seg + 1)
                store_seg(seg - 1, l_before)
                load_seg(seg, l, g)

            mod_in(0)
            mod(0, 0)
            mod_rows_in(0)
            x_in(0, CTX)
            mod_out(0, 0)
            bc_in(0, CTX)
            even_in(CTX)
            mod(0, 1)
            kv_out()
            mod_out(0, 1)
            out_in(0, CTX)
            prep(0, CTX)
            mix_in(0, SMP)
            prep_end(0, CTX)
            even_in(SMP)
            out_in(0, SMP)
            prep(0, SMP)
            store_seg(0, 0)
            load_seg(1, 0, SMP)
            prep_end(0, SMP)
            load_h(2)
            mod_in(1)
            for part in range(2):
                mod(1, part)
                if part == 0:
                    mod_rows_in(1)
            for part in range(2):
                mod_out(1, part)
            with Segments(sp, 2, 4, per_seg) as seg:
                segment(seg, 0, SMP, 0)
            mix_in(1, CTX)
            store_seg(3, 0)
            load_seg(4, 0, SMP)
            odd_in(CTX)
            out_in(1, CTX)
            prep(1, CTX)
            load_h(5)
            prep_end(1, CTX)
            store_seg(4, 0)
            load_seg(5, 1, CTX)
            mix_in(1, SMP)
            odd_in(SMP)
            out_in(1, SMP)
            prep(1, SMP)
            store_seg(5, 1)
            load_seg(6, 1, SMP)
            load_h(7)
            with Segments(sp, 7, 9, per_seg) as seg:
                segment(seg, 1, SMP, 1)
            store_seg(8, 1)
            load_seg(9, 1, SMP)
            store_seg(9, 1)

        @block.gpsimd
        def _(pool):
            per_seg = {(dots_done, ""): (128, 1 - NU), (vsum_done, ""): (128, 1 - NV - TOPK), (topk_done, ""): (8, 1)}
            u_rows = T["peer_u"].rearrange("l e d -> (l e) d")
            v_rows = T["peer_v"].rearrange("l e d -> (l e) d")

            def gather_u(i, h, k):
                wait(pool, dots_done, 16 * i + k - NU + 1)
                pool.indirect_dma_start(out=u_ring[:, k % NU, :], out_offset=None, in_=u_rows,
                                        in_offset=bass.IndirectOffsetOnAxis(ap=idx[:, h % 4, k:k + 1], axis=0)
                                        ).then_inc(u_landed[k % NU], 16)

            def gather_v(i, h, k):
                before = 16 * i + k - NV
                if isinstance(before, int) and before >= 0 and by_vector(before // ROWS, before % ROWS):
                    pool.wait_ge(vector_sum, vector_count(before + 1))
                else:
                    wait(pool, vsum_done, before + 1)
                pool.indirect_dma_start(out=v_ring[:, k % NV, :], out_offset=None, in_=v_rows,
                                        in_offset=bass.IndirectOffsetOnAxis(ap=idx[:, h % 4, k:k + 1], axis=0)
                                        ).then_inc(v_landed[k % NV], 16)

            def step(seg, h, first=False):
                i = seg * 8 + h
                wait(pool, topk_done, i + 1)
                for k in range(TOPK):
                    gather_u(i, h, k)
                    if not first:
                        gather_v(i - 1, h - 1, k)

            for i in range(16):
                step(i // 8, i % 8, first=i == 0)
            with Segments(pool, 2, 4, per_seg) as seg:
                for h in range(HEADS):
                    step(seg, h)
            for i in range(32, 56):
                step(i // 8, i % 8)
            with Segments(pool, 7, 9, per_seg) as seg:
                for h in range(HEADS):
                    step(seg, h)
            for h in range(HEADS):
                step(9, h)
            for k in range(TOPK):
                gather_v(79, 7, k)

        @block.tensor
        def _(pe):
            per_seg = {(acc_free, ""): (1, 0), (diag_done, ""): (128, 1 - TOPK), **{(s, ""): (256, -16) for s in v_landed}}
            pe.wait_ge(const_in, 64)

            place = [0, 0]

            def rows(n):
                for _ in range(n):
                    seg, r = place
                    place[1] += 1
                    if behind(seg, r) is None:
                        continue
                    seg, r = behind(seg, r)
                    v = seg * ROWS + r
                    if by_vector(seg, r):
                        continue
                    if r == 0:
                        wait(pe, acc_free, seg)
                    wait(pe, diag_done, v + 1)
                    wait(pe, v_landed[r % NV], seg * (2 * ROWS) + 16 * (r // NV) + 16)
                    for half in range(2):
                        last = nc.tensor.matmul(ps_v[:, 512 * half:512 * half + 512], diag[:, r % NDIAG, :],
                                                v_ring[:, r % NV, 512 * half:512 * half + 512],
                                                start=(r == 0), stop=(r == ROWS - 1))
                    last.then_inc(vsum_done, 1)

            def start(seg):
                assert seg == 0 or place[1] == ROWS
                place[:] = [seg, 0]

            def cond(l):
                pe.wait_ge(S("cond_in", l), 32)
                box = fill(pe, ("condT", l))
                filled(nc.tensor.transpose(box[:, 0:16], cond_raw, ident[0:16, 0:16]), ("condT", l))
                given(pe, ("condT", l))

            def mod_slices(l, part, box, lo, hi):
                ct = cond_t(l).rearrange("p (g c) -> p c g", g=2)
                first, end = MOD_SLICES[part]
                for s in range(lo, hi):
                    w = weight(pe, ("wmod", l, s))
                    for j in range(2):
                        at = 2 * (2 * (s - first) + j)
                        for c in range(DC):
                            last = nc.tensor.matmul(box[:, at:at + 2], w[:, c, j * P:(j + 1) * P],
                                                    ct[:, c, :], start=(c == 0), stop=(c == DC - 1))
                    last.then_inc(S("wmod_read", l), 1)
                    if l:
                        rows(MOD_RATE)

            def mod_turn(l, part):
                n = 4 * (MOD_SLICES[part][1] - MOD_SLICES[part][0])
                pe.wait_ge(S("mod_sb", l), part + 1)
                box = fill(pe, ("modT", l, part))
                filled(nc.tensor.transpose(box[0:n, 0:P], mod_at(l, part, "sb"), ident[:, :]), ("modT", l, part))

            def cw_turn(l, g):
                rows = CW_ROWS if l == 0 else 3
                pe.wait_ge(S("cw_in", l, g), 16 * (4 if l == 0 else 1))
                box = fill(pe, ("cwT", l, g))
                for c in range(4):
                    last = nc.tensor.transpose(box[:, c * rows:(c + 1) * rows], cw_raw[0:rows, c * P:(c + 1) * P],
                                               ident[0:rows, 0:rows])
                filled(last, ("cwT", l, g))

            def turn_h(l, g, name, ready):
                for b in range(len(BLOCKS[g])):
                    pe.wait_ge(S(ready, l, g), b + 1)
                    box = fill(pe, (name, l, g, b))
                    src = h_tile(b) if name == "hT" else XM[:, b, :]
                    for c in range(DC):
                        last = nc.tensor.transpose(box[:, c * P:(c + 1) * P], src[:, c * P:(c + 1) * P], ident[:, :])
                    filled(last, (name, l, g, b))
                    rows(rate(l, g, "norm"))

            def proj_t(out, w, col, g):
                h = ht(g)
                for c in range(DC):
                    last = nc.tensor.matmul(out, w[:, c, col:col + P], h[:, c, :], start=(c == 0), stop=(c == DC - 1))
                return last

            def even_a(g):
                t, nb = tokens(g), len(BLOCKS[g])
                given(pe, ("hT", 0, g, nb - 1))
                for c in range(4):
                    wv = weight(pe, ("win", 0, g, c // 2))
                    wg = weight(pe, ("win", 0, g, 2 + c // 2))
                    box = fill(pe, ("vg", g, c))
                    proj_t(box[:, 512:512 + t], wg, (c % 2) * P, g)
                    filled(proj_t(box[:, 0:t], wv, (c % 2) * P, g), ("vg", g, c))
                    rows(rate(0, g, "vg"))
                rows(rate(0, g, "vg_end"))

            def even_qkv(g):
                nb = len(BLOCKS[g])
                h = ht(g)
                if g == SMP:
                    pe.wait_ge(S("cache_dup"), 1)
                    box = fill(pe, ("ckT", g))
                    for v in range(2):
                        last = nc.tensor.transpose(box[:, v * P:(v + 1) * P], kdup[:, v * P:(v + 1) * P], ident[:, :])
                    filled(last, ("ckT", g))

                def project(b):
                    box = fill(pe, ("qkv", g, b))
                    for s in range(3):
                        w = weight(pe, ("win", 0, g, 4 + s))
                        for c in range(DC):
                            last = nc.tensor.matmul(box[:, s * WC:(s + 1) * WC], h[:, c, b * P:(b + 1) * P], w[:, c, :],
                                                    start=(c == 0), stop=(c == DC - 1))
                    filled(last, ("qkv", g, b))

                project(0)
                for b in range(nb):
                    if b + 1 < nb:
                        project(b + 1)
                    rows(rate(0, g, "qkv"))
                    pe.wait_ge(S("rot", g), b + 1)
                    box = fill(pe, ("qkT", g, b))
                    for c in range(4):
                        nc.tensor.transpose(box[:, c * P:(c + 1) * P], rot[:, c * P:(c + 1) * P], ident[:, :])
                    for v in range(2):
                        last = nc.tensor.transpose(box[:, 512 + v * P:512 + (v + 1) * P], kdup[:, v * P:(v + 1) * P], ident[:, :])
                    filled(last, ("qkT", g, b))

            def attend(g, b, beside=lambda h: None):
                nk = n_keys(g)
                q, k = q_t(g), k_t(g)
                given(pe, ("qkT", g, len(BLOCKS[g]) - 1))

                def score(h):
                    lo = HD * (h % 2)
                    box = fill(pe, ("S", g, b, h))
                    for at in range(0, nk, 512):
                        to = min(nk, at + 512)
                        last = nc.tensor.matmul(box[:, at:to], q[lo:lo + HD, h // 2, b * P:(b + 1) * P],
                                                k[lo:lo + HD, h // 4, at:to], start=True, stop=True)
                    filled(last, ("S", g, b, h))

                score(0)
                for h in range(HEADS):
                    if h < HEADS - 1:
                        score(h + 1)
                    given(pe, ("S", g, b, h))
                    box = fill(pe, ("PT", g, b, h))
                    for kb in range(nk // P):
                        last = nc.tensor.transpose(box[:, kb * P:(kb + 1) * P], prob[:, kb * P:(kb + 1) * P], ident[:, :])
                    filled(last, ("PT", g, b, h))
                    rows(rate(0, g, "attend"))
                    beside(h)
                    given(pe, ("PT", g, b, h))
                    box = fill(pe, ("O", g, b, h))
                    for kb in range(nk // P):
                        last = nc.tensor.matmul(box[:, 0:HD], prob_t[:, kb, :], v_t[:, kb, HD * (h // 4):HD * (h // 4) + HD],
                                                start=(kb == 0), stop=(kb == nk // P - 1))
                    filled(last, ("O", g, b, h))
                given(pe, ("O", g, b, 7))
                box = fill(pe, ("oT", g, b))
                for c in range(4):
                    last = nc.tensor.transpose(box[:, c * P:(c + 1) * P], o_tok[:, c * P:(c + 1) * P], ident[:, :])
                filled(last, ("oT", g, b))

            def conv_norm(g):
                t = tokens(g)
                pe.wait_ge(S("conv", g), 4 * CONVK)
                for key, src, ready in (("mean", conv_out(g), None), ("var", conv_sq(g), "conv_sq")):
                    if ready:
                        pe.wait_ge(S(ready, g), 1)
                    box = fill(pe, (key, g))
                    for c in range(4):
                        last = nc.tensor.matmul(box[:, 0:t], ones[:, :], src[:, c, :], start=(c == 0), stop=(c == 3))
                    filled(last, (key, g))
                    rows(rate(0, g, "conv_norm") // 2)

            def odd_a(g):
                t, nb = tokens(g), len(BLOCKS[g])
                given(pe, ("hT", 1, g, nb - 1))
                for c in range(4):
                    w = weight(pe, ("win", 1, g, c // 2))
                    box = fill(pe, ("fT", g, c))
                    filled(proj_t(box[:, 0:t], w, (c % 2) * P, g), ("fT", g, c))
                    rows(rate(1, g, "f"))
                rows(rate(1, g, "f_end"))
                for c in range(4):
                    box = fill(pe, ("cv", g, c))
                    proj_t(box[:, 0:t], weight(pe, ("win", 1, g, 4 + c // 2)), (c % 2) * P, g)
                    last = proj_t(box[:, 512:512 + t], weight(pe, ("win", 1, g, 6 + c // 2)), (c % 2) * P, g)
                    filled(last, ("cv", g, c))
                    rows(rate(1, g, "cv") // 2)
                    box = fill(pe, ("gb", g, c))
                    filled(proj_t(box[:, 0:t], weight(pe, ("win", 1, g, 2 + c // 2)), (c % 2) * P, g), ("gb", g, c))
                    rows(rate(1, g, "cv") // 2)
                    if c == 1:
                        rows(rate(1, g, "cv_end"))

            def odd_fft(g):
                t, nb = tokens(g), len(BLOCKS[g])
                f, y = f_t(g), y_tok(g)
                given(pe, ("fT", g, 3))
                for b in range(nb):
                    box = fill(pe, ("Y", g, b))
                    for c in range(4):
                        last = nc.tensor.matmul(box[:, c * 256:(c + 1) * 256], f[:, c, b * P:(b + 1) * P], dft_ch[:, :],
                                                start=True, stop=True)
                    filled(last, ("Y", g, b))
                    rows(rate(1, g, "Y"))
                given(pe, ("Y", g, nb - 1))
                pe.wait_ge(S("dft_in", g), 16)
                d = dft_t(g)
                for c in range(4):
                    box = fill(pe, ("ffT", g, c))
                    for b in range(nb):
                        for s in range(2):
                            last = nc.tensor.matmul(box[:, 0:t], y[:, b, c, s * P:(s + 1) * P], d[:, s, b, :],
                                                    start=(b == 0 and s == 0), stop=(b == nb - 1 and s == 1))
                    filled(last, ("ffT", g, c))
                    rows(rate(1, g, "ff"))

            def mix_out(l, g):
                nb = len(BLOCKS[g])
                x = cat(g)
                if l == 0:
                    pe.wait_ge(S("cat_a", g), 4)
                    given(pe, ("oT", g, nb - 1))
                else:
                    given(pe, ("gb", g, 3))
                    given(pe, ("ffT", g, 3))
                for s in range(4):
                    w = weight(pe, ("wout", l, g, s))
                    for b in range(nb):
                        box = fill(pe, ("out", l, g, s, b))
                        for c in range(8):
                            last = nc.tensor.matmul(box[:, 0:WC], x[:, c, b * P:(b + 1) * P], w[:, c, :],
                                                    start=(c == 0), stop=(c == 7))
                        filled(last, ("out", l, g, s, b))
                        rows(rate(l, g, "out"))
                rows(rate(l, g, "out_end"))

            def scores(l, g, lo=0, hi=8):
                nb = len(BLOCKS[g])
                t = tokens(g)
                given(pe, ("h2T", l, g, nb - 1))
                for s in range(lo, hi):
                    w = weight(pe, ("wq", l, g, s))
                    kr = weight_keys(("wq", l, g, s))
                    box = fill(pe, ("kyT", l, g, s))
                    for j in range(2):
                        last = nc.tensor.transpose(box[:, j * P:(j + 1) * P], kr[:, j, :], ident[:, :])
                    filled(last, ("kyT", l, g, s))
                    for j in range(2):
                        box = fill(pe, ("q", l, g, 2 * s + j))
                        filled(proj_t(box[:, 0:t], w, j * P, g), ("q", l, g, 2 * s + j))
                        rows(rate(l, g, "slice") // 2)
                    given(pe, ("kyT", l, g, s))
                    for j in range(2):
                        n = 2 * s + j
                        given(pe, ("q", l, g, n))
                        box = fill(pe, ("sc", l, g, n))
                        for b in range(nb):
                            last = nc.tensor.matmul(box[:, b * P:(b + 1) * P], q_sb(g, j)[:, b * P:(b + 1) * P], ky_sb[:, j, :],
                                                    start=True, stop=True)
                        filled(last, ("sc", l, g, n))

            cond(0)
            mod_slices(0, 0, ps_v, *MOD_SLICES[0])
            nc.tensor.matmul(ps_v[:, 512:514], ident[:, :], ident[:, 0:2], start=True, stop=True).then_inc(S("mod_sums", 0), 1)
            mod_turn(0, 0)
            cw_turn(0, CTX)
            turn_h(0, CTX, "hT", "h_tok")
            even_a(CTX)
            even_qkv(CTX)
            lo, hi = MOD_SLICES[1]
            attend(CTX, 0, lambda h: mod_slices(0, 1, ps_v, lo + 2 * h, lo + 2 * h + 2))
            nc.tensor.matmul(ps_v[:, 512:514], ident[:, :], ident[:, 0:2], start=True, stop=True).then_inc(S("mod_sums", 0), 1)
            mod_turn(0, 1)
            conv_norm(CTX)
            mix_out(0, CTX)
            turn_h(0, CTX, "h2T", "h2_tok")
            scores(0, CTX, 0, 2)
            start(0)
            scores(0, CTX, 2, 8)
            rows(TOPK)
            cw_turn(0, SMP)
            turn_h(0, SMP, "hT", "h_tok")
            even_a(SMP)
            even_qkv(SMP)
            for b in range(4):
                attend(SMP, b)
            conv_norm(SMP)
            mix_out(0, SMP)
            turn_h(0, SMP, "h2T", "h2_tok")
            scores(0, SMP, 0, 2)
            rows(ROWS - place[1])
            start(1)
            scores(0, SMP, 2, 4)
            rows(TOPK - place[1])
            for s in range(4, 8):
                scores(0, SMP, s, s + 1)
                rows(TOPK * (s - 2) - place[1])
            cond(1)
            for part in range(2):
                box = fill(pe, ("mod", 1, part))
                mod_slices(1, part, box, *MOD_SLICES[part])
                filled(nc.tensor.matmul(box[:, 512:514], ident[:, :], ident[:, 0:2], start=True, stop=True), ("mod", 1, part))
                mod_turn(1, part)
            rows(ROWS - place[1])
            with Segments(pe, 2, 4, per_seg) as seg:
                start(seg)
                rows(ROWS)
            start(4)
            rows(TOPK)
            cw_turn(1, CTX)
            turn_h(1, CTX, "hT", "h_tok")
            odd_a(CTX)
            odd_fft(CTX)
            mix_out(1, CTX)
            turn_h(1, CTX, "h2T", "h2_tok")
            scores(1, CTX)
            rows(ROWS - place[1])
            start(5)
            rows(TOPK + rate(1, SMP, "start"))
            cw_turn(1, SMP)
            turn_h(1, SMP, "hT", "h_tok")
            odd_a(SMP)
            odd_fft(SMP)
            mix_out(1, SMP)
            turn_h(1, SMP, "h2T", "h2_tok")
            scores(1, SMP, 0, 2)
            rows(ROWS - place[1])
            start(6)
            scores(1, SMP, 2, 4)
            rows(TOPK - place[1])
            for s in range(4, 8):
                scores(1, SMP, s, s + 1)
                rows(TOPK * (s - 2) - place[1])
            rows(ROWS - place[1])
            with Segments(pe, 7, 9, per_seg) as seg:
                start(seg)
                rows(ROWS)
            start(9)
            rows(ROWS)
            start(10)
            rows(TOPK)

        @block.scalar
        def _(act):
            per_seg = {(w_done, "diags"): (8, 0), (w_done, "gelu"): (8, -1), (w_done, "exps"): (8, -1),
                      (vsum_done, ""): (128, 1 - NDIAG - TOPK), (dots_done, ""): (128, 16), (negmax_done, ""): (8, 3), (topk_done, ""): (8, 2),
                      (h_landed, ""): (16, 32), (x_new, ""): (1, 0)}
            chain = Chain(act, act_chain)
            act.wait_ge(const_in, 64)
            act.wait_ge(S("ones_set"), 1)

            place = [0, 0]

            def diagonal(seg, r):
                if behind(seg, r) is None:
                    return
                seg, r = behind(seg, r)
                h, k = r // TOPK, r % TOPK
                if by_vector(seg, r):
                    return
                if k == 0:
                    wait(act, w_done, seg * HEADS + h + 1, "diags")
                wait(act, vsum_done, seg * ROWS + r - NDIAG + 1)
                nc.scalar.activation(diag[:, k % NDIAG, :], ident[:, :], ACT.Copy,
                                     scale=w_v[:, h % 2, k:k + 1]).then_inc(diag_done, 1)

            def gelu(seg, h):
                i = seg * 8 + h
                wait(act, w_done, i - 1, "gelu")
                wait(act, dots_done, 16 * i + 16)
                nc.scalar.activation(gelu_v[:, h % 2, :], act_v[:, h % 2, :], ACT.Gelu_apprx_tanh).then_inc(gelu_done, 1)

            def exps(seg, h):
                i = seg * 8 + h
                wait(act, negmax_done, i + 1)
                wait(act, w_done, i - 3, "exps")
                nc.scalar.activation(ex[:, h % 4, :], fv[:, h % 2, :], ACT.Exp, bias=neg_max[:, h % 2:h % 2 + 1],
                                     accum_out=ex_sum[:, h % 4:h % 4 + 1]).then_inc(exp_done, 1)

            def take_h(seg):
                wait(act, h_landed, 16 * seg + 16)
                nc.scalar.activation(h_cur[:, :], h_next[:, :], ACT.Copy).then_inc(h_ready, 1)

            def seg_square(seg):
                wait(act, x_new, seg + 1)
                chain(nc.scalar.activation(t_seg[:, :], x_seg[:, :], ACT.Square, accum_out=seg_st[:, 0:1]))
                nc.scalar.activation(seg_st[:, 1:2], seg_st[:, 0:1], ACT.Sqrt, bias=eps[:, 0:1], scale=1.0 / D).then_inc(ss_done, 1)

            def load_s(seg, h):
                i = seg * 8 + h
                wait(act, topk_done, i - 1)
                act.dma_start(s_buf[:, h % 2], sc[index(i)]).then_inc(s_landed[h % 2], 16)

            def rows(n):
                for _ in range(n):
                    seg, r = place
                    place[1] += 1
                    diagonal(seg, r)
                    if r % TOPK != TOPK - 1:
                        continue
                    h = r // TOPK
                    last = isinstance(seg, int) and seg == 9
                    held = isinstance(seg, int) and seg in (0, 5)
                    gelu(seg, h)
                    if h == 0 and (seg if isinstance(seg, int) else seg.loop.lo) >= 6:
                        seg_square(seg - 1)
                    if h == 7 and not last:
                        take_h(seg + 1)
                    if h < 6 or not (last or held):
                        exps(seg + (h + 2) // 8, (h + 2) % 8)
                    if h < 5 or not (last or held):
                        load_s(seg + (h + 3) // 8, (h + 3) % 8)

            def start(seg):
                assert seg == 0 or place[1] == ROWS
                place[:] = [seg, 0]

            def cond(l):
                give(nc.scalar.activation(cond_t(l), take(act, ("condT", l))[:, 0:16], ACT.Silu), ("condT", l))

            def mod(l, part):
                if l == 0:
                    act.wait_ge(S("mod_sums", 0), part + 1)
                    box = ps_v
                else:
                    box = take(act, ("mod", l, part))
                n = 4 * (MOD_SLICES[part][1] - MOD_SLICES[part][0])
                turned = nc.scalar.activation(mod_at(l, part, "sb").rearrange("p (g j) -> p g j", g=2),
                                              box[:, 0:n].rearrange("p (j g) -> p g j", g=2), ACT.Copy)
                turned.then_inc(S("mod_sb", l), 1)
                if l:
                    act.wait_ge(S("mod_sb", l), part + 1)
                    act.sem_inc(box_free[boxes[("mod", l, part)][0]], 1)

            def cw_sb(l, g):
                rows = CW_ROWS if l == 0 else 3
                box = take(act, ("cwT", l, g))
                dst = cw if l == 0 else cw_odd
                act.wait_ge(S("xm_in", l, g), 16 * len(BLOCKS[g]))
                give(nc.scalar.activation(dst, box[:, 0:4 * rows].rearrange("p (c r) -> p c r", c=4), ACT.Copy), ("cwT", l, g))

            def norm(l, g, name):
                nb = len(BLOCKS[g])
                at = 0 if name == "hT" else 12
                if name == "hT":
                    act.wait_ge(S("xm_in", l, g), 16 * nb)
                else:
                    act.wait_ge(S("x_mixed", l, g), 1)
                for b in range(nb):
                    if name == "hT" and b >= 2:
                        box, use = boxes[("hT", l, g, b - 2)]
                        act.wait_ge(box_ready[box], use + 1)
                    chain(nc.scalar.activation(h_tile(b), XM[:, b, :], ACT.Square, accum_out=st[:, at + b:at + b + 1]))
                    nc.scalar.activation(st[:, at + 4 + b:at + 5 + b], st[:, at + b:at + b + 1], ACT.Sqrt, bias=eps[:, 0:1],
                                         scale=1.0 / D).then_inc(S("rms", name, l, g), 1)
                    if b >= 1:
                        h_sb(l, g, name, b - 1)
                        rows(rate(l, g, "norm"))
                h_sb(l, g, name, nb - 1)
                rows(rate(l, g, "norm"))

            def h_sb(l, g, name, b):
                box = take(act, (name, l, g, b))
                give(nc.scalar.activation(ht(g)[:, :, b * P:(b + 1) * P], box[:, :].rearrange("p (c t) -> p c t", c=8), ACT.Copy),
                     (name, l, g, b))

            def even_a(g):
                t = tokens(g)
                for c in range(4):
                    box = take(act, ("vg", g, c))
                    if c >= 2:
                        given(act, ("vg", g, c - 2))
                    nc.scalar.activation(small(c)[:, 0:t], box[:, 512:512 + t], ACT.Sigmoid).then_inc(S("sig", g), 1)
                    rows(rate(0, g, "vg"))
                rows(rate(0, g, "vg_end"))

            def even_qkv(g):
                off = 1 if g == SMP else 0
                if g == SMP:
                    box = take(act, ("ckT", g))
                    give(nc.scalar.activation(k_t(g)[:, :, 0:P], box[:, 0:256].rearrange("p (v t) -> p v t", v=2), ACT.Copy), ("ckT", g))
                for b in range(len(BLOCKS[g])):
                    box = take(act, ("qkv", g, b))
                    if b:
                        act.wait_ge(S("rot", g), b)
                    elif g == SMP:
                        act.wait_ge(S("cache_dup"), 1)
                    nc.scalar.activation(raw[:, 0:QK], box[:, 0:QK], ACT.Copy)
                    give(nc.scalar.activation(v_t[:, b + off, :], box[:, QK:QK + P], ACT.Copy), ("qkv", g, b))
                    rows(rate(0, g, "qkv"))
                    act.wait_ge(S("qk_ss", g), b + 1)
                    nc.scalar.activation(st[:, 34:44], st[:, 24:34], ACT.Sqrt, bias=eps[:, 0:1], scale=1.0 / HD).then_inc(S("qk_rms", g), 1)
                    box = take(act, ("qkT", g, b))
                    nc.scalar.activation(q_t(g)[:, :, b * P:(b + 1) * P], box[:, 0:512].rearrange("p (c t) -> p c t", c=4), ACT.Copy)
                    give(nc.scalar.activation(k_t(g)[:, :, (b + off) * P:(b + off + 1) * P],
                                              box[:, 512:768].rearrange("p (v t) -> p v t", v=2), ACT.Copy), ("qkT", g, b))

            def attend(g, b):
                nk = n_keys(g)
                for h in range(HEADS):
                    n = b * HEADS + h
                    box = take(act, ("S", g, b, h))
                    act.wait_ge(S("row_max", g), n + 1)
                    if n:
                        bx, use = boxes[("PT", g, (n - 1) // 8, (n - 1) % 8)]
                        act.wait_ge(box_ready[bx], use + 1)
                    give(nc.scalar.activation(prob[:, 0:nk], box[:, 0:nk], ACT.Exp, bias=st[:, 46 + n % 2:47 + n % 2],
                                              scale=HD ** -0.5, accum_out=st[:, 52 + n % 4:53 + n % 4]), ("S", g, b, h))
                    box = take(act, ("PT", g, b, h))
                    if n:
                        bx, use = boxes[("O", g, (n - 1) // 8, (n - 1) % 8)]
                        act.wait_ge(box_ready[bx], use + 1)
                    give(nc.scalar.activation(prob_t[:, 0:nk // P, :], box[:, 0:nk].rearrange("p (b n) -> p b n", n=P), ACT.Copy),
                         ("PT", g, b, h))
                    rows(rate(0, g, "attend"))
                box = take(act, ("oT", g, b))
                give(nc.scalar.activation(cat(g)[:, 4:8, b * P:(b + 1) * P], box[:, 0:512].rearrange("p (c t) -> p c t", c=4), ACT.Copy),
                     ("oT", g, b))

            def conv_norm(g):
                t = tokens(g)
                given(act, ("mean", g))
                nc.scalar.activation(conv_sq(g), conv_out(g), ACT.Square).then_inc(S("conv_sq", g), 1)
                rows(rate(0, g, "conv_norm") // 2)
                box = take(act, ("var", g))
                give(nc.scalar.activation(small(1)[:, 0:t], box[:, 0:t], ACT.Sqrt, bias=eps[:, 0:1]), ("var", g))
                rows(rate(0, g, "conv_norm") // 2)
                act.wait_ge(S("conv_unit", g), 1)
                for c in range(4):
                    nc.scalar.activation(cat(g)[:, c, :], conv_out(g)[:, c, :], ACT.Silu, scale=cw[:, c, CONVK + 1:CONVK + 2],
                                         bias=cw[:, c, CONVK + 2:CONVK + 3]).then_inc(S("cat_a", g), 1)

            def odd_a(g):
                t = tokens(g)
                for c in range(4):
                    box = take(act, ("fT", g, c))
                    give(nc.scalar.activation(f_t(g)[:, c, :], box[:, 0:t], ACT.Copy), ("fT", g, c))
                    rows(rate(1, g, "f"))
                rows(rate(1, g, "f_end"))
                for c in range(4):
                    box = take(act, ("cv", g, c))
                    if c:
                        given(act, ("cv", g, c - 1))
                    nc.scalar.activation(gc_sb[:, 0:t], box[:, 0:t], ACT.Copy).then_inc(S("gc", g), 1)
                    rows(rate(1, g, "cv"))
                    if c == 1:
                        rows(rate(1, g, "cv_end"))

            def odd_fft(g):
                t = tokens(g)
                for b in range(len(BLOCKS[g])):
                    box = take(act, ("Y", g, b))
                    give(nc.scalar.activation(y_tok(g)[:, b].rearrange("p c n -> p (c n)"), box[:, :], ACT.Copy), ("Y", g, b))
                    rows(rate(1, g, "Y"))
                for c in range(4):
                    box = take(act, ("ffT", g, c))
                    give(nc.scalar.activation(cat(g)[:, c, :], box[:, 0:t], ACT.Copy), ("ffT", g, c))
                    rows(rate(1, g, "ff"))

            def mix_out(l, g):
                rows(rate(l, g, "out") * 4 * len(BLOCKS[g]) + rate(l, g, "out_end"))

            def scores(l, g, lo=0, hi=8):
                t, nb = tokens(g), len(BLOCKS[g])
                for s in range(lo, hi):
                    box = take(act, ("kyT", l, g, s))
                    give(nc.scalar.activation(ky_sb, box[:, 0:256].rearrange("p (j k) -> p j k", j=2), ACT.Copy), ("kyT", l, g, s))
                    for j in range(2):
                        box = take(act, ("q", l, g, 2 * s + j))
                        give(nc.scalar.activation(q_sb(g, j), box[:, 0:t], ACT.Copy), ("q", l, g, 2 * s + j))
                        rows(rate(l, g, "slice") // 2)
                    for j in range(2):
                        n = 2 * s + j
                        box = take(act, ("sc", l, g, n))
                        if j == 0 and s >= 2:
                            stored(act, l, g, s - 2)
                        give(nc.scalar.activation(stage(g, s % 2)[:, :, j, :], box[:, 0:t].rearrange("p (b k) -> p b k", b=nb),
                                                  ACT.Copy), ("sc", l, g, n))
                    given(act, ("sc", l, g, 2 * s + 1))
                    for b in range(nb):
                        act.dma_start(sc[8 * seg_of(l, g, b) + s].rearrange("p j k -> p (j k)"),
                                      stage(g, s % 2)[:, b].rearrange("p j k -> p (j k)")).then_inc(S("stage_out", l, g, s % 2), 16)

            def enter(seg, l, g):
                scores(l, g, 0, 2)
                rows(rate(l, g, "enter") // 2)
                for h in range(2):
                    stored(act, l, g, h)
                    load_s(seg, h)
                rows(rate(l, g, "enter") // 2)
                exps(seg, 0)
                if seg:
                    rows(max(0, 7 * TOPK - place[1]))
                exps(seg, 1)

            def third(seg, l, g):
                scores(l, g, 2, 3)
                stored(act, l, g, 2)
                load_s(seg, 2)
                scores(l, g, 3, 4)
                stored(act, l, g, 3)

            cond(0)
            mod(0, 0)
            cw_sb(0, CTX)
            norm(0, CTX, "hT")
            even_a(CTX)
            even_qkv(CTX)
            attend(CTX, 0)
            mod(0, 1)
            conv_norm(CTX)
            norm(0, CTX, "h2T")
            enter(0, 0, CTX)
            take_h(0)
            start(0)
            third(0, 0, CTX)
            scores(0, CTX, 4, 8)
            rows(TOPK)
            for h in (6, 7):
                stored(act, 0, CTX, h)
            cw_sb(0, SMP)
            norm(0, SMP, "hT")
            even_a(SMP)
            even_qkv(SMP)
            for b in range(4):
                attend(SMP, b)
            conv_norm(SMP)
            mix_out(0, SMP)
            norm(0, SMP, "h2T")
            enter(1, 0, SMP)
            rows(ROWS - place[1])
            start(1)
            third(1, 0, SMP)
            rows(TOPK - place[1])
            for s in range(4, 8):
                scores(0, SMP, s, s + 1)
                stored(act, 0, SMP, s)
                rows(TOPK * (s - 2) - place[1])
            cond(1)
            for part in range(2):
                rows(MOD_RATE * (MOD_SLICES[part][1] - MOD_SLICES[part][0]))
                mod(1, part)
            rows(ROWS - place[1])
            with Segments(act, 2, 4, per_seg) as seg:
                chain.restart()
                start(seg)
                rows(ROWS)
            start(4)
            rows(TOPK)
            cw_sb(1, CTX)
            norm(1, CTX, "hT")
            odd_a(CTX)
            odd_fft(CTX)
            mix_out(1, CTX)
            norm(1, CTX, "h2T")
            scores(1, CTX)
            for h in (6, 7):
                stored(act, 1, CTX, h)
            rows(ROWS - place[1])
            start(5)
            rows(TOPK + rate(1, SMP, "start"))
            cw_sb(1, SMP)
            norm(1, SMP, "hT")
            odd_a(SMP)
            odd_fft(SMP)
            mix_out(1, SMP)
            norm(1, SMP, "h2T")
            enter(6, 1, SMP)
            rows(ROWS - place[1])
            start(6)
            third(6, 1, SMP)
            rows(TOPK - place[1])
            for s in range(4, 8):
                scores(1, SMP, s, s + 1)
                stored(act, 1, SMP, s)
                rows(TOPK * (s - 2) - place[1])
            rows(ROWS - place[1])
            with Segments(act, 7, 9, per_seg) as seg:
                chain.restart()
                start(seg)
                rows(ROWS)
            start(9)
            rows(ROWS)
            for r in range(TOPK):
                diagonal(10, r)
            seg_square(9)

        @block.vector
        def _(dve):
            per_seg = {(h_ready, ""): (1, 1), (s_landed[0], ""): (64, 32), (s_landed[1], ""): (64, 32), (exp_done, "topk"): (8, 1),
                      (exp_done, "weigh"): (8, 1), (vsum_done, "end"): (128, 0), (vsum_done, "idx"): (128, -16),
                      (gelu_done, ""): (8, 1), (diag_done, ""): (128, -16), (seg_landed, ""): (32, 0), (acc_free, ""): (1, 0),
                      (ss_done, ""): (1, -5), **{(s, ""): (256, 16) for s in u_landed}}
            chain = Chain(dve, dve_chain)
            nc.vector.memset(eps[:, :], EPS)
            nc.vector.memset(ones[:, :], 1.0 / 512).then_inc(S("ones_set"), 1)
            dve.wait_ge(const_in, 64)

            place = [0, 0]

            def dot(seg, r):
                h, k = r // TOPK, r % TOPK
                if r == 0:
                    wait(dve, h_ready, seg + 1)
                wait(dve, u_landed[k % NU], seg * (2 * ROWS) + 16 * (r // NU) + 16)
                nc.vector.tensor_tensor_reduce(u_ring[:, k % NU, :], u_ring[:, k % NU, :], h_cur[:, :], 1.0, 0.0,
                                               ALU.mult, ALU.add, act_v[:, h % 2, k:k + 1]).then_inc(dots_done, 1)

            def add_v(seg, r):
                h, k = r // TOPK, r % TOPK
                n = VECTOR_ROWS.index((seg, r))
                dve.wait_ge(w_done, seg * HEADS + h + 1)
                dve.wait_ge(v_landed[k % NV], seg * (2 * ROWS) + 16 * (r // NV) + 16)
                row, weight = v_ring[:, k % NV, :], w_v[:, h % 2, k:k + 1]
                if h == 0 and k == VECTOR_RANKS[0]:
                    ins = nc.vector.tensor_scalar(v_acc(seg), row, weight, None, ALU.mult)
                else:
                    dve.wait_ge(vector_sum, n)
                    ins = nc.vector.scalar_tensor_tensor(v_acc(seg), row, weight, v_acc(seg), ALU.mult, ALU.add)
                ins.then_inc(vector_sum, 1)

            def fold(seg, n):
                dve.wait_ge(vector_sum, n)
                dve.wait_ge(seg_landed, 32 * seg + 32)
                chain(nc.vector.tensor_tensor(v_acc(seg), v_acc(seg), g_seg[:, :], ALU.mult))
                chain(nc.vector.tensor_tensor(x_seg[:, :], x_seg[:, :], v_acc(seg), ALU.add))

            def top16(values, indices, src, rep):
                chain(nc.vector.max(values[:, 0:8], src))
                nc.vector.max_index(indices[:, 0:8], values[:, 0:8], src)
                chain(nc.vector.match_replace(rep, values[:, 0:8], src, NEG))
                chain(nc.vector.max(values[:, 8:16], rep))
                chain(nc.vector.max_index(indices[:, 8:16], values[:, 8:16], rep))

            def topk(seg, h):
                i = seg * 8 + h
                l = seg // 5 if isinstance(seg, int) else seg.loop.lo // 5
                wait(dve, s_landed[h % 2], 64 * seg + 16 * (h // 2) + 16)
                wait(dve, exp_done, i - 1, "topk")
                for j in range(2):
                    top16(sv[:, j, :], si[:, j, :], s_buf[:, h % 2, j, :], s_rep[:, j, :])
                chain(nc.vector.tensor_tensor(cand[:, :, :], sv[:, 0, :].unsqueeze(2).to_broadcast([P, 16, 16]),
                                              sv[:, 1, :].unsqueeze(1).to_broadcast([P, 16, 16]), ALU.add))
                flat = cand[:, :, :].rearrange("p a b -> p (a b)")
                top16(fv[:, h % 2, :], fi[:, :], flat, cand_rep)
                nc.vector.tensor_scalar(neg_max[:, h % 2:h % 2 + 1], fv[:, h % 2, 0:1], -1.0, None, ALU.mult).then_inc(negmax_done, 1)
                nc.vector.tensor_scalar(ab[:, 0, :], fi[:, :], 4, None, ALU.logical_shift_right)
                chain(nc.vector.tensor_scalar(ab[:, 1, :], fi[:, :], 15, None, ALU.bitwise_and))
                nc.vector.tensor_copy(sif[:, :, :], si[:, :, :])
                chain(nc.vector.tensor_copy(abf[:, :, :], ab[:, :, :]))
                for j in range(2):
                    last = nc.vector.tensor_tensor(onehot[:, j], abf[:, j, :].unsqueeze(2).to_broadcast([P, 16, 16]),
                                                   iota16[:, :].unsqueeze(1).to_broadcast([P, 16, 16]), ALU.is_equal)
                chain(last)
                for j in range(2):
                    last = nc.vector.tensor_tensor(onehot[:, j], onehot[:, j],
                                                   sif[:, j, :].unsqueeze(1).to_broadcast([P, 16, 16]), ALU.mult)
                chain(last)
                chain(nc.vector.tensor_reduce(e01[:, :, :], onehot[:, :, :, :], AX, ALU.add))
                chain(nc.vector.scalar_tensor_tensor(e01[:, 0, :], e01[:, 0, :], float(KEYS), e01[:, 1, :], ALU.mult, ALU.add))
                wait(dve, vsum_done, 16 * (i - 3), "idx")
                nc.vector.tensor_scalar(idx[:, h % 4, :], e01[:, 0, :], float(l * EXPERTS), None, ALU.add).then_inc(topk_done, 1)

            def weigh(seg, h):
                i = seg * 8 + h
                wait(dve, exp_done, i + 1, "weigh")
                chain(nc.vector.reciprocal(ex_rec[:, h % 4:h % 4 + 1], ex_sum[:, h % 4:h % 4 + 1]))
                wait(dve, gelu_done, i + 1)
                wait(dve, diag_done, 16 * (i - 1))
                nc.vector.scalar_tensor_tensor(w_v[:, h % 2, :], gelu_v[:, h % 2, :], ex_rec[:, h % 4:h % 4 + 1], ex[:, h % 4, :],
                                               ALU.mult, ALU.mult).then_inc(w_done, 1)

            def seg_end(seg, l):
                wait(dve, vsum_done, 128 * seg + 128, "end")
                wait(dve, seg_landed, 32 * seg + 32)
                nc.vector.tensor_tensor(t_seg[:, :], ps_v[:, :], g_seg[:, :], ALU.mult).then_inc(acc_free, 1)
                wait(dve, acc_free, seg + 1)
                nc.vector.tensor_tensor(x_seg[:, :], x_seg[:, :], t_seg[:, :], ALU.add).then_inc(x_new, 1)
                if l == 1:
                    dve.wait_ge(fg_landed, 16)
                    wait(dve, ss_done, seg - 4)
                    chain(nc.vector.reciprocal(seg_st[:, 2:3], seg_st[:, 1:2]))
                    nc.vector.scalar_tensor_tensor(t_seg[:, :], x_seg[:, :], seg_st[:, 2:3], BC[:, 0, :], ALU.mult,
                                                   ALU.mult).then_inc(y_new, 1)

            def rows(n):
                for _ in range(n):
                    seg, r = place
                    place[1] += 1
                    dot(seg, r)
                    v_row = behind(seg, r)
                    if v_row and by_vector(*v_row):
                        add_v(*v_row)
                        if v_row == VECTOR_ROWS[-1] or v_row[0] != VECTOR_ROWS[VECTOR_ROWS.index(v_row) + 1][0]:
                            fold(v_row[0], VECTOR_ROWS.index(v_row) + 1)
                    if r % TOPK != TOPK - 1:
                        continue
                    h = r // TOPK
                    static = isinstance(seg, int)
                    if h == 0 and not (static and seg == 0):
                        seg_end(seg - 1, int(seg > 5) if static else seg.loop.lo // 5)
                    if h < 6 or not (static and seg in (0, 5, 9)):
                        topk(seg + (h + 2) // 8, (h + 2) % 8)
                    weigh(seg, h)

            def start(seg):
                assert seg == 0 or place[1] == ROWS
                place[:] = [seg, 0]

            def mod_gain(l):
                for part in range(2):
                    nc.vector.memset(mod_at(l, part, "gain"), 1.0).then_inc(S("gain_one", l), 1)

            def mod(l, part):
                n = 4 * (MOD_SLICES[part][1] - MOD_SLICES[part][0])
                row = mod_at(l, part, "row")
                dve.wait_ge(S("mod_in", l), 16 * 10)
                box = take(dve, ("modT", l, part))
                give(nc.vector.tensor_tensor(row, box[0:n, 0:P], mod_at(l, part, "bias"), ALU.add), ("modT", l, part))
                given(dve, ("modT", l, part))
                nc.vector.scalar_tensor_tensor(row, row, mod_at(l, part, "mask"), mod_at(l, part, "gain"), ALU.add,
                                               ALU.mult).then_inc(S("mod_row", l), 1)

            def norm(l, g, name):
                nb = len(BLOCKS[g])
                at = 0 if name == "hT" else 12
                if name == "hT":
                    dve.wait_ge(S("bc_in", l, g), 32)
                else:
                    dve.wait_ge(S("bc_ffn", l, g), 32)
                    dve.wait_ge(S("xa_out", l, g), 16 * nb)
                for b in range(nb):
                    dve.wait_ge(S("rms", name, l, g), b + 1)
                    r = st[:, at + 8 + b:at + 9 + b]
                    chain(nc.vector.reciprocal(r, st[:, at + 4 + b:at + 5 + b]))
                    dst = h_tile(b) if name == "hT" else XM[:, b, :]
                    chain(nc.vector.scalar_tensor_tensor(dst, XM[:, b, :], r, BC[:, 0, :], ALU.mult, ALU.mult))
                    nc.vector.tensor_tensor(dst, dst, BC[:, 1, :], ALU.add).then_inc(S("h_tok" if name == "hT" else "h2_tok", l, g), 1)
                    rows(rate(l, g, "norm"))

            def even_a(g):
                t = tokens(g)
                u = conv_u(g)
                nc.vector.memset(u[:, :, 0:PAD], 0.0)
                nc.vector.memset(u[:, :, PAD + t:], 0.0)
                for c in range(4):
                    dve.wait_ge(S("sig", g), c + 1)
                    box = take(dve, ("vg", g, c))
                    give(nc.vector.tensor_tensor(u[:, c, PAD:PAD + t], box[:, 0:t], small(c)[:, 0:t], ALU.mult), ("vg", g, c))
                    rows(rate(0, g, "vg"))
                rows(rate(0, g, "vg_end"))

            def heads(ap, n=10):
                return ap.rearrange("p (h d) -> p h d", h=n)

            def dup(src, g):
                dst = kdup.rearrange("p (v e d) -> p v e d", v=2, e=2)
                for e in range(2):
                    last = nc.vector.tensor_copy(dst[:, :, e, :], src.rearrange("p (v d) -> p v d", v=2))
                return last

            def even_qkv(g):
                dve.wait_ge(S("gain_in", g), 160)
                if g == SMP:
                    dve.wait_ge(S("cache_in"), 32)
                    dup(raw[:, 512:640], g).then_inc(S("cache_dup"), 1)
                    box, use = boxes[("ckT", g)]
                    dve.wait_ge(box_ready[box], use + 1)
                for b in range(len(BLOCKS[g])):
                    given(dve, ("qkv", g, b))
                    chain(nc.vector.tensor_tensor(nrm, raw[:, 0:QK], raw[:, 0:QK], ALU.mult))
                    nc.vector.tensor_reduce(st[:, 24:34], heads(nrm), AX, ALU.add).then_inc(S("qk_ss", g), 1)
                    rows(rate(0, g, "qkv"))
                    dve.wait_ge(S("qk_rms", g), b + 1)
                    chain(nc.vector.reciprocal(st[:, 24:34], st[:, 34:44]))
                    chain(nc.vector.tensor_tensor(heads(nrm), heads(raw[:, 0:QK]), st[:, 24:34].unsqueeze(2).to_broadcast([P, 10, HD]), ALU.mult))
                    if b:
                        box, use = boxes[("qkT", g, b - 1)]
                        dve.wait_ge(box_ready[box], use + 1)
                    if g == CTX:
                        chain(nc.vector.tensor_tensor(rot, nrm, gain, ALU.mult))
                    else:
                        chain(nc.vector.tensor_tensor(nrm, nrm, gain, ALU.mult))
                        pair = nrm.rearrange("p (h d e) -> p h d e", h=10, e=2)
                        out = rot.rearrange("p (h d e) -> p h d e", h=10, e=2)
                        cos = rope[:, b, 0, :].unsqueeze(1).to_broadcast([P, 10, 32])
                        sin = rope[:, b, 1, :].unsqueeze(1).to_broadcast([P, 10, 32])
                        for e, (m1, m2, op) in enumerate(((cos, sin, ALU.subtract), (sin, cos, ALU.add))):
                            nc.vector.tensor_tensor(heads(rt1), pair[:, :, :, 0], m1, ALU.mult)
                            chain(nc.vector.tensor_tensor(heads(rt2), pair[:, :, :, 1], m2, ALU.mult))
                            chain(nc.vector.tensor_tensor(out[:, :, :, e], heads(rt1), heads(rt2), op))
                    dup(rot[:, 512:640], g).then_inc(S("rot", g), 1)

            def conv(g, lo, hi):
                t = tokens(g)
                u, out = conv_u(g), conv_out(g)
                if lo == 0:
                    given(dve, ("vg", g, 3))
                    given(dve, ("cwT", 0, g))
                    box, use = boxes[("qkv", g, len(BLOCKS[g]) - 1)]
                    dve.wait_ge(box_ready[box], use + 1)
                for j in range(lo, hi):
                    for c in range(4):
                        if j == 0:
                            ins = nc.vector.tensor_scalar(out[:, c, :], u[:, c, 0:t], cw[:, c, 0:1], cw[:, c, CONVK:CONVK + 1],
                                                          ALU.mult, ALU.add)
                        else:
                            dve.wait_ge(S("conv", g), 4 * j + c - 3)
                            ins = nc.vector.scalar_tensor_tensor(out[:, c, :], u[:, c, j:j + t], cw[:, c, j:j + 1], out[:, c, :],
                                                                 ALU.mult, ALU.add)
                        ins.then_inc(S("conv", g), 1)

            def attend(g, b, taps):
                nk = n_keys(g)

                def row_max(h):
                    n = b * HEADS + h
                    box = take(dve, ("S", g, b, h))
                    chain(nc.vector.tensor_reduce(st[:, 44 + n % 2:45 + n % 2], box[:, 0:nk], AX, ALU.max))
                    nc.vector.tensor_scalar(st[:, 46 + n % 2:47 + n % 2], st[:, 44 + n % 2:45 + n % 2], -HD ** -0.5, None,
                                            ALU.mult).then_inc(S("row_max", g), 1)

                row_max(0)
                for h in range(HEADS):
                    n = b * HEADS + h
                    if h < HEADS - 1:
                        row_max(h + 1)
                    rows(rate(0, g, "attend"))
                    lo = taps[0] + (taps[1] - taps[0]) * h // HEADS
                    hi = taps[0] + (taps[1] - taps[0]) * (h + 1) // HEADS
                    conv(g, lo, hi)
                    given(dve, ("S", g, b, h))
                    chain(nc.vector.reciprocal(st[:, 56 + n % 4:57 + n % 4], st[:, 52 + n % 4:53 + n % 4]))
                    box = take(dve, ("O", g, b, h))
                    if h == 0 and b:
                        bx, use = boxes[("oT", g, b - 1)]
                        dve.wait_ge(box_ready[bx], use + 1)
                    give(nc.vector.tensor_scalar(o_tok[:, h * HD:(h + 1) * HD], box[:, 0:HD], st[:, 56 + n % 4:57 + n % 4], None,
                                                 ALU.mult), ("O", g, b, h))

            def conv_norm(g):
                t = tokens(g)
                out = conv_out(g)
                box = take(dve, ("mean", g))
                dve.wait_ge(S("conv", g), 4 * CONVK)
                give(nc.vector.tensor_tensor(out, out, box[:, 0:t].unsqueeze(1).to_broadcast([P, 4, t]), ALU.subtract), ("mean", g))
                rows(rate(0, g, "conv_norm") // 2)
                given(dve, ("var", g))
                chain(nc.vector.reciprocal(small(0)[:, 0:t], small(1)[:, 0:t]))
                nc.vector.tensor_tensor(out, out, small(0)[:, 0:t].unsqueeze(1).to_broadcast([P, 4, t]), ALU.mult).then_inc(S("conv_unit", g), 1)
                rows(rate(0, g, "conv_norm") // 2)

            def odd_a(g):
                t = tokens(g)
                given(dve, ("cwT", 1, g))
                nc.vector.memset(s_pad[:, 0:1], 0.0)
                chain(nc.vector.memset(s_pad[:, t + 1:t + 2], 0.0))
                for c in range(4):
                    dve.wait_ge(S("gc", g), c + 1)
                    box = take(dve, ("cv", g, c))
                    give(nc.vector.tensor_tensor(s_pad[:, 1:t + 1], gc_sb[:, 0:t], box[:, 512:512 + t], ALU.mult), ("cv", g, c))
                    given(dve, ("cv", g, c))
                    rows(rate(1, g, "cv") // 2)
                    dst = cat(g)[:, 4 + c, :]
                    chain(nc.vector.tensor_scalar(dst, s_pad[:, 0:t], cw_odd[:, c, 0:1], None, ALU.mult))
                    for j in (1, 2):
                        chain(nc.vector.scalar_tensor_tensor(dst, s_pad[:, j:j + t], cw_odd[:, c, j:j + 1], dst, ALU.mult, ALU.add))
                    box = take(dve, ("gb", g, c))
                    give(nc.vector.tensor_tensor(dst, dst, box[:, 0:t], ALU.mult), ("gb", g, c))
                    rows(rate(1, g, "cv") // 2)
                    if c == 1:
                        rows(rate(1, g, "cv_end"))

            def others(n):
                rows(n)

            def scores(l, g, lo, hi):
                rows(rate(l, g, "slice") * (hi - lo))

            def mix_out(l, g):
                nb = len(BLOCKS[g])
                dve.wait_ge(S("bc_gate", l, g), 16)
                n = 0
                for s in range(4):
                    for b in range(nb):
                        box = take(dve, ("out", l, g, s, b))
                        tmp = small(n)[:, 0:WC]
                        give(nc.vector.tensor_tensor(tmp, box[:, 0:WC], BC[:, 0, s * WC:(s + 1) * WC], ALU.mult), ("out", l, g, s, b))
                        given(dve, ("out", l, g, s, b))
                        x = XM[:, b, s * WC:(s + 1) * WC]
                        last = nc.vector.tensor_tensor(x, x, tmp, ALU.add)
                        n += 1
                        if n < 4 * nb:
                            chain(last)
                            rows(rate(l, g, "out"))
                last.then_inc(S("x_mixed", l, g), 1)
                rows(rate(l, g, "out") + rate(l, g, "out_end"))

            mod_gain(0)
            mod(0, 0)
            norm(0, CTX, "hT")
            even_a(CTX)
            even_qkv(CTX)
            attend(CTX, 0, (0, CONVK))
            mod(0, 1)
            conv_norm(CTX)
            mix_out(0, CTX)
            norm(0, CTX, "h2T")
            topk(0, 0)
            topk(0, 1)
            start(0)
            rows(TOPK)
            norm(0, SMP, "hT")
            even_a(SMP)
            even_qkv(SMP)
            for b in range(4):
                attend(SMP, b, (8 * b, min(8 * b + 8, CONVK)))
            conv_norm(SMP)
            mix_out(0, SMP)
            norm(0, SMP, "h2T")
            scores(0, SMP, 0, 2)
            rows(rate(0, SMP, "enter"))
            topk(1, 0)
            rows(max(0, 7 * TOPK - place[1]))
            topk(1, 1)
            rows(ROWS - place[1])
            start(1)
            rows(5 * TOPK)
            mod_gain(1)
            rows(MOD_RATE * MOD_SLICES[0][1])
            mod(1, 0)
            rows(MOD_RATE * (MOD_SLICES[1][1] - MOD_SLICES[1][0]))
            mod(1, 1)
            rows(ROWS - place[1])
            with Segments(dve, 2, 4, per_seg) as seg:
                chain.restart()
                start(seg)
                rows(ROWS)
            start(4)
            rows(TOPK)
            norm(1, CTX, "hT")
            others(4 * rate(1, CTX, "f"))
            odd_a(CTX)
            others(rate(1, CTX, "Y") + 4 * rate(1, CTX, "ff"))
            mix_out(1, CTX)
            norm(1, CTX, "h2T")
            scores(1, CTX, 0, 8)
            rows(ROWS - place[1])
            start(5)
            rows(TOPK + rate(1, SMP, "start"))
            norm(1, SMP, "hT")
            others(4 * rate(1, SMP, "f") + rate(1, SMP, "f_end"))
            odd_a(SMP)
            others(4 * rate(1, SMP, "Y") + 4 * rate(1, SMP, "ff"))
            mix_out(1, SMP)
            norm(1, SMP, "h2T")
            scores(1, SMP, 0, 2)
            rows(rate(1, SMP, "enter"))
            topk(6, 0)
            rows(max(0, 7 * TOPK - place[1]))
            topk(6, 1)
            rows(ROWS - place[1])
            start(6)
            rows(ROWS)
            with Segments(dve, 7, 9, per_seg) as seg:
                chain.restart()
                start(seg)
                rows(ROWS)
            start(9)
            rows(ROWS)
            seg_end(9, 1)


_INS = ["x_prompt", "x_sample", "cache_k", "cache_v", "c", "c_ctx", "w_mod", "b_mod", "norm_mix_g", "norm_ffn_g",
        "w_in_even", "w_out_even", "conv_dw_w", "conv_dw_b", "conv_ln_g", "conv_ln_b", "q_norm_g", "k_norm_g",
        "w_in_odd", "w_out_odd", "short_conv_w", "peer_wq", "peer_keys", "peer_u", "peer_v", "final_norm_g"]
_OUTS = [(1, P, D), (1, 4 * P, D), (1, 1, P, 2, HD), (1, 1, P, 2, HD)]


def shape_tables():
    def dft(n):
        a = 2 * np.pi * (np.outer(np.arange(n), np.arange(n)) % n) / n
        return np.cos(a) / np.sqrt(n), np.sin(a) / np.sqrt(n)

    c, s = dft(P)
    out = {"ident": np.eye(P), "dft_ch": np.concatenate([c, s], 1), "iota16": np.tile(np.arange(16.0), (P, 1))}
    for name, n in (("dft_ctx", P), ("dft_smp", 4 * P)):
        c, s = dft(n)
        out[name] = np.stack([c, -s]).reshape(2, n // P, P, n).transpose(2, 0, 1, 3)
    grid_w, half, theta = 64, HD // 2, 10000.0
    inv = np.float32(theta) ** (-np.arange(0, half, 2, dtype=np.float32) / half)
    t = np.arange(4 * P)
    ang = np.concatenate([(t // grid_w).astype(np.float32)[:, None] * inv, (t % grid_w).astype(np.float32)[:, None] * inv], 1)
    r = np.stack([np.cos(ang), np.sin(ang)], 1)
    out["rope"] = r.reshape(4, P, 2, half).transpose(1, 0, 2, 3)
    for part, n, scale in ((0, 2, 1), (1, 4, 2)):
        mask = np.zeros((2, n, 8))
        mask[:, scale] = 1.0
        out[f"scale_rows{part}"] = mask.reshape(-1, 1)
    return {k: np.ascontiguousarray(v.astype(np.float32)) for k, v in out.items()}


def kernel(**inputs):
    import numpy as _np
    import concourse.bacc as _bacc
    from concourse import mybir as _mybir
    from concourse.bass_utils import run_bass_kernel_spmd as _run

    nc = _bacc.Bacc("TRN2", target_bir_lowering=False, num_devices=1)
    arrays, args = {}, {}
    given = {name: _np.ascontiguousarray(inputs[name]) for name in _INS}
    for name, a in list(given.items()) + list(shape_tables().items()):
        arrays[f"in_{name}_dram"] = a
        args[name] = nc.dram_tensor(f"in_{name}_dram", a.shape, _mybir.dt.from_np(a.dtype), kind="ExternalInput").ap()
    outs = [nc.dram_tensor(f"out_{i}_dram", shape, _mybir.dt.float32, kind="ExternalOutput").ap()
            for i, shape in enumerate(_OUTS)]
    build(nc, args, outs)
    r = _run(nc, [arrays], core_ids=[0])
    return tuple(r.results[0][f"out_{i}_dram"] for i in range(len(_OUTS)))
```
